# Optimizing a Trainium2 kernel written in Bass

```python
import math
import jax, jax.numpy as jnp
from jax import lax
import numpy as np

D_MODEL = 1024
BATCH = 1
SEQ = 512
DEPTH = 2

ATT_HEADS = 8
HEAD_DIM = 64
ATT_WIDTH = ATT_HEADS * HEAD_DIM
MOBA_BLOCK = 256
MOBA_TOPK = 3
Q_CHUNK = 128
POOL_WINDOWS = (2, 4, 8, 16)
POOL_GROUPS = 4
POOL_WIDTH = D_MODEL - ATT_WIDTH
POOL_GROUP_DIM = POOL_WIDTH // POOL_GROUPS
EVEN_IN = 3 * ATT_WIDTH + POOL_WIDTH
CONV_WIDTH = 3
ODD_IN = 3 * D_MODEL
D_FF = 2816
N_EVEN = (DEPTH + 1) // 2
N_ODD = DEPTH // 2
DN_ALPHA = (2 * DEPTH) ** 0.25
DN_BETA = (8 * DEPTH) ** -0.25
LN_EPS = 1e-5
NEG = -1e30

kernel_name = "moba_pool_shortconv_deepnorm_hybrid"

def layer_norm(x, g, b):
    xf = x.astype(jnp.float32)
    mu = jnp.mean(xf, axis=-1, keepdims=True)
    var = jnp.mean(jnp.square(xf - mu), axis=-1, keepdims=True)
    return ((xf - mu) * lax.rsqrt(var + LN_EPS)).astype(x.dtype) * g + b

def causal_dwconv(u, w, b):
    K, C = w.shape
    y = lax.conv_general_dilated(
        u, w[:, None, :].astype(u.dtype), window_strides=(1,), padding=[(K - 1, 0)],
        dimension_numbers=('NWC', 'WIO', 'NWC'), feature_group_count=C)
    return y + b

def moba_attention(q, k, v):
    Bn, S, H, Dh = q.shape
    nb = -(-S // MOBA_BLOCK)
    s_pad = nb * MOBA_BLOCK
    k_top = min(MOBA_TOPK, nb)
    qh = q.transpose(0, 2, 1, 3)
    pad = ((0, 0), (0, 0), (0, s_pad - S), (0, 0))
    kb = jnp.pad(k.transpose(0, 2, 1, 3), pad).reshape(Bn, H, nb, MOBA_BLOCK, Dh)
    vb = jnp.pad(v.transpose(0, 2, 1, 3), pad).reshape(Bn, H, nb, MOBA_BLOCK, Dh)
    kmean = jnp.mean(kb.astype(jnp.float32), axis=3)
    scale = Dh ** -0.5
    b_ix = jnp.arange(Bn)[:, None, None]
    h_ix = jnp.arange(H)[None, :, None]
    blk_ids = jnp.arange(nb)
    in_blk = jnp.arange(MOBA_BLOCK)

    def chunk(c):
        q0 = c * Q_CHUNK
        qc = lax.dynamic_slice_in_dim(qh, q0, Q_CHUNK, axis=2).astype(jnp.float32) * scale
        qpos = q0 + jnp.arange(Q_CHUNK)
        blk = q0 // MOBA_BLOCK
        gate = jnp.einsum('bhqd,bhnd->bhqn', qc, kmean)
        gate = jnp.where(blk_ids < blk, gate, NEG)
        _, sel = lax.top_k(gate, k_top)
        k_own = lax.dynamic_index_in_dim(kb, blk, axis=2, keepdims=False)
        v_own = lax.dynamic_index_in_dim(vb, blk, axis=2, keepdims=False)
        kpos = blk * MOBA_BLOCK + in_blk
        s_own = jnp.einsum('bhqd,bhkd->bhqk', qc, k_own.astype(jnp.float32))
        scores = [jnp.where(kpos[None, :] <= qpos[:, None], s_own, NEG)]
        for j in range(k_top):
            k_j = kb[b_ix, h_ix, sel[..., j]]
            s_j = jnp.einsum('bhqd,bhqkd->bhqk', qc, k_j.astype(jnp.float32))
            scores.append(jnp.where(j < blk, s_j, NEG))
        p = jax.nn.softmax(jnp.concatenate(scores, axis=-1), axis=-1)
        p = p.reshape(Bn, H, Q_CHUNK, 1 + k_top, MOBA_BLOCK)
        out = jnp.einsum('bhqk,bhkd->bhqd', p[..., 0, :], v_own.astype(jnp.float32))
        for j in range(k_top):
            v_j = vb[b_ix, h_ix, sel[..., j]]
            out = out + jnp.einsum('bhqk,bhqkd->bhqd', p[..., j + 1, :], v_j.astype(jnp.float32))
        return out.astype(v.dtype)

    o = lax.map(chunk, jnp.arange(S // Q_CHUNK))
    return o.transpose(1, 0, 3, 2, 4).reshape(Bn, S, H * Dh)

def multiscale_pool(u, w_pool, b_pool, pool_scale):
    Bn, S, _ = u.shape
    uf = u.astype(jnp.float32).reshape(Bn, S, POOL_GROUPS, POOL_GROUP_DIM)
    cs = jnp.concatenate([jnp.zeros_like(uf[:, :1]), jnp.cumsum(uf, axis=1)], axis=1)
    win = jnp.array(POOL_WINDOWS, dtype=jnp.int32)
    t = jnp.arange(S, dtype=jnp.int32)[:, None]
    g = jnp.arange(POOL_GROUPS, dtype=jnp.int32)[None, :]
    lo = jnp.maximum(t + 1 - win[None, :], 0)
    window_sum = cs[:, t + 1, g] - cs[:, lo, g]
    count = jnp.minimum(t + 1, win[None, :]).astype(jnp.float32)
    pooled = (window_sum / count[None, :, :, None] - uf).astype(u.dtype)
    mixed = jnp.einsum('bsgc,gcd->bsgd', pooled, w_pool) + b_pool
    return mixed.reshape(Bn, S, POOL_WIDTH) * pool_scale

def attn_pool_mixer(x, w_in, w_pool, b_pool, pool_scale, w_out):
    Bn, S, _ = x.shape
    h = x @ w_in
    q, k, v, u = jnp.split(h, [ATT_WIDTH, 2 * ATT_WIDTH, 3 * ATT_WIDTH], axis=-1)
    shp = (Bn, S, ATT_HEADS, HEAD_DIM)
    a = moba_attention(q.reshape(shp), k.reshape(shp), v.reshape(shp))
    p = multiscale_pool(u, w_pool.reshape(POOL_GROUPS, POOL_GROUP_DIM, POOL_GROUP_DIM),
                        b_pool.reshape(POOL_GROUPS, POOL_GROUP_DIM), pool_scale)
    return jnp.concatenate([a, p], axis=-1) @ w_out

def short_conv_mixer(x, w_in, conv_w, conv_b, w_out):
    b_gate, c_gate, hval = jnp.split(x @ w_in, 3, axis=-1)
    return (b_gate * causal_dwconv(c_gate * hval, conv_w, conv_b)) @ w_out

def conv_glu_ffn(x, w_up, conv_w, conv_b, w_down):
    gu = causal_dwconv(x @ w_up, conv_w, conv_b)
    g, u = jnp.split(gu, 2, axis=-1)
    return (jax.nn.silu(g) * u) @ w_down

def setup_inputs(seed: int = 0) -> dict:
    key = jax.random.key(seed)
    ks = jax.random.split(key, 24)
    f32 = jnp.float32
    nrm = lambda k, shp, s: jax.random.normal(k, shp, f32) * s
    L = DEPTH
    return {
        "x": nrm(ks[0], (BATCH, SEQ, D_MODEL), 1.0),
        "even_w_in": nrm(ks[1], (N_EVEN, D_MODEL, EVEN_IN), D_MODEL ** -0.5),
        "even_w_pool": nrm(ks[2], (N_EVEN, POOL_GROUPS * POOL_GROUP_DIM, POOL_GROUP_DIM), POOL_GROUP_DIM ** -0.5),
        "even_b_pool": nrm(ks[3], (N_EVEN, POOL_WIDTH), 0.02),
        "even_pool_scale": 1.0 + nrm(ks[4], (N_EVEN, POOL_WIDTH), 0.02),
        "even_w_out": nrm(ks[5], (N_EVEN, D_MODEL, D_MODEL), DN_BETA * D_MODEL ** -0.5),
        "odd_w_in": nrm(ks[6], (N_ODD, D_MODEL, ODD_IN), D_MODEL ** -0.5),
        "odd_conv_w": nrm(ks[7], (N_ODD, CONV_WIDTH, D_MODEL), CONV_WIDTH ** -0.5),
        "odd_conv_b": nrm(ks[8], (N_ODD, D_MODEL), 0.02),
        "odd_w_out": nrm(ks[9], (N_ODD, D_MODEL, D_MODEL), DN_BETA * D_MODEL ** -0.5),
        "mix_ln_g": 1.0 + nrm(ks[10], (L, D_MODEL), 0.02),
        "mix_ln_b": nrm(ks[11], (L, D_MODEL), 0.02),
        "ffn_w_up": nrm(ks[12], (L, D_MODEL, 2 * D_FF), D_MODEL ** -0.5),
        "ffn_conv_w": nrm(ks[13], (L, CONV_WIDTH, 2 * D_FF), CONV_WIDTH ** -0.5),
        "ffn_conv_b": nrm(ks[14], (L, 2 * D_FF), 0.02),
        "ffn_w_down": nrm(ks[15], (L, D_FF, D_MODEL), DN_BETA * D_FF ** -0.5),
        "ffn_ln_g": 1.0 + nrm(ks[16], (L, D_MODEL), 0.02),
        "ffn_ln_b": nrm(ks[17], (L, D_MODEL), 0.02),
    }

def reference(x, even_w_in, even_w_pool, even_b_pool, even_pool_scale, even_w_out,
              odd_w_in, odd_conv_w, odd_conv_b, odd_w_out,
              mix_ln_g, mix_ln_b, ffn_w_up, ffn_conv_w, ffn_conv_b, ffn_w_down,
              ffn_ln_g, ffn_ln_b):
    for l in range(DEPTH):
        i = l // 2
        if l % 2 == 0:
            m = attn_pool_mixer(x, even_w_in[i], even_w_pool[i], even_b_pool[i],
                                even_pool_scale[i], even_w_out[i])
        else:
            m = short_conv_mixer(x, odd_w_in[i], odd_conv_w[i], odd_conv_b[i], odd_w_out[i])
        x = layer_norm(DN_ALPHA * x + m, mix_ln_g[l], mix_ln_b[l])
        f = conv_glu_ffn(x, ffn_w_up[l], ffn_conv_w[l], ffn_conv_b[l], ffn_w_down[l])
        x = layer_norm(DN_ALPHA * x + f, ffn_ln_g[l], ffn_ln_b[l])
    return x


_drawn_inputs = setup_inputs


def setup_inputs(seed=0):
    import zlib

    import numpy as np

    out = dict(_drawn_inputs(seed))
    spreads = {}
    factors = {'even_b_pool': 8.0, 'even_pool_scale': 22.953, 'odd_conv_b': 8.0, 'ffn_conv_b': 6.269}
    for name, (base, spread) in spreads.items():
        noise = np.random.default_rng([zlib.crc32(name.encode()), seed]).standard_normal(out[name].shape)
        drawn = base * np.exp(spread * noise) if base else spread * noise
        out[name] = __import__('jax').numpy.asarray(drawn.astype(out[name].dtype))
    for name, factor in factors.items():
        out[name] = (out[name] * factor).astype(out[name].dtype)
    return out
```

```python
from contextlib import ExitStack

import concourse.bass as bass
from concourse import mybir

ALU = mybir.AluOpType
ACT = mybir.ActivationFunctionType
F32 = mybir.dt.float32
F32R = mybir.dt.float32r
BF16 = mybir.dt.bfloat16
AX_X = mybir.AxisListType.X
P = 128


def trunk_program(nc, x_in, even_w_in, even_w_pool, even_b_pool, even_pool_scale, even_w_out,
                  odd_w_in, odd_conv_w, odd_conv_b, odd_w_out, mix_ln_g, mix_ln_b,
                  ffn_w_up, ffn_conv_w, ffn_conv_b, ffn_w_down, ffn_ln_g, ffn_ln_b, out):
    _, SEQ, D = x_in.shape
    DEPTH = mix_ln_g.shape[0]
    DFF = ffn_w_down.shape[1]
    ATT = D // 2
    HEAD_DIM = 64
    ST = SEQ // P
    DC = D // P
    FC = DFF // P
    AC = ATT // P
    GROUPS = AC
    ALPHA = float((2 * DEPTH) ** 0.25)
    EPS = 1e-5
    NEG = -1e30
    SCALE = float(HEAD_DIM) ** -0.5
    RING = 4
    TAIL = 4
    PAD = 8
    ACC = 4 + 4
    assert (SEQ, D, DEPTH, FC % 2) == (512, 1024, 2, 0)

    U_POOLIN, U_Q, U_K, U_V = 0, 4, 8, 12
    U_OUT0 = 16
    U_UP0 = U_OUT0 + DC
    U_DOWN0 = U_UP0 + 2 * FC
    U_CH = U_DOWN0 + FC
    U_B = U_CH + 2 * DC
    U_OUT1 = U_B + DC
    U_UP1 = U_OUT1 + DC
    U_DOWN1 = U_UP1 + 2 * FC
    UNITS = U_DOWN1 + FC

    FREE_UP0 = 12
    FREE_CH = FREE_UP0 + 2 * FC
    FREE_UP1 = FREE_CH + 2 * DC
    FREE_END = FREE_UP1 + 2 * FC
    H_OUT0 = 0
    H_DOWN0 = H_OUT0 + DC
    H_OUT1 = H_DOWN0 + FC
    H_DOWN1 = H_OUT1 + DC
    CONV_UP0, CONV_CH, CONV_UP1 = 0, 2 * FC, 2 * FC + DC

    SLOT_K, SLOT_Q, SLOT_V = DC, DC + AC, DC + 2 * AC

    NF = 2 * FC

    def col_ffn(layer, tap):
        return (layer * 4 + tap) * NF
    COL_BPOOL = DEPTH * 4 * NF
    COL_PSCALE = COL_BPOOL + GROUPS
    COL_ODDW = COL_PSCALE + GROUPS
    COL_ODDB = COL_ODDW + 3 * DC
    COLS = COL_ODDB + DC

    with ExitStack() as ctx:
        def sb(name, shape, dt=F32):
            return ctx.enter_context(nc.sbuf_tensor(name, shape, dt))

        def sem(name):
            return ctx.enter_context(nc.semaphore(name))

        ps = ctx.enter_context(nc.psum_tensor("ps", [P, ACC, 512], F32))

        w_raw = sb("w_raw", [P, RING, D])
        w_hi = sb("w_hi", [P, RING, D], F32R)
        w_lo = sb("w_lo", [P, RING, D], F32R)
        xt_hi = sb("xt_hi", [P, DC, SEQ], F32R)
        xt_lo = sb("xt_lo", [P, DC, SEQ], F32R)
        x = sb("x", [P, ST, D])
        h = sb("h", [P, FC, SEQ])
        ht_hi = sb("ht_hi", [P, RING, SEQ], F32R)
        ht_lo = sb("ht_lo", [P, RING, SEQ], F32R)
        gb = sb("gb", [P, 2, D])
        conv = sb("conv", [P, 2, 2, SEQ])
        act_g = sb("act_g", [P, 2, SEQ])
        probs = sb("probs", [P, 2, 1280])
        probs_t = sb("probs_t", [P, 1280])
        o_nat = sb("o_nat", [P, ST, ATT])
        q_pad = sb("q_pad", [P, 2, SEQ])
        wpool = sb("wpool", [P, GROUPS, P])
        table = sb("table", [P, COLS])
        ident = sb("ident", [P, P])
        ident_b = sb("ident_b", [P, P], BF16)
        mask_b = sb("mask_b", [P, P], BF16)
        inv_count = sb("inv_count", [P, 16])
        stats = sb("stats", [P, 6, ST])
        neg_half = sb("neg_half", [P, 1])
        att_stat = sb("att_stat", [P, 3, 2, ST])

        pool_buf = probs[:, :, :].rearrange("p a b -> p (a b)")[:, 0:3 * (PAD + SEQ)].rearrange(
            "p (a b) -> p a b", a=3)
        rows = probs[:, :, :].rearrange("p a b -> p (a b)")[:, 3 * (PAD + SEQ):3 * (PAD + SEQ) + 5 * P].rearrange(
            "p (a b) -> p a b", a=5)
        pooled = o_nat

        zsum, nmu, vsum, var, rstd = (stats[:, i, :] for i in range(5))
        neg_max, prob_sum, prob_inv = (att_stat[:, i, :, :] for i in range(3))

        raw_loaded = [sem(f"raw_loaded{i}") for i in range(RING)]
        x_loaded = [sem(f"x_loaded{i}") for i in range(ST)]
        rows_loaded = sem("rows_loaded")
        wpool_loaded = sem("wpool_loaded")
        gb_loaded = sem("gb_loaded")
        out_stored = sem("out_stored")
        const_set = sem("const_set")
        const_ready = sem("const_ready")
        inv_ready = sem("inv_ready")
        hi_ready = sem("hi_ready")
        split_ready = sem("split_ready")
        unit_done = sem("unit_done")
        bank_free = sem("bank_free")
        table_t = sem("table_t")
        table_ready = sem("table_ready")
        xt_ps = sem("xt_ps")
        xt_hi_ready = sem("xt_hi_ready")
        xt_ready = sem("xt_ready")
        h_ready = sem("h_ready")
        ht_hi_ready = sem("ht_hi_ready")
        ht_ready = sem("ht_ready")
        pool_step = sem("pool_step")
        pooled_ready = sem("pooled_ready")
        mixed_done = sem("mixed_done")
        v_ready = sem("v_ready")
        v_dve = sem("v_dve")
        q_staged = sem("q_staged")
        scores_done = sem("scores_done")
        max_ready = sem("max_ready")
        probs_ready = sem("probs_ready")
        pt_done = sem("pt_done")
        pt_act = sem("pt_act")
        pt_dve = sem("pt_dve")
        o_done = sem("o_done")
        inv_sum = sem("inv_sum")
        o_ready = sem("o_ready")
        ot_done = sem("ot_done")
        conv_base = sem("conv_base")
        tap1 = sem("tap1")
        gate_ready = sem("gate_ready")
        c_ready = sem("c_ready")
        short_ready = sem("short_ready")
        tile_done = sem("tile_done")
        z_ready = sem("z_ready")
        mu_ready = sem("mu_ready")
        sq_ready = sem("sq_ready")
        var_ready = sem("var_ready")
        rstd_ready = sem("rstd_ready")
        xg_ready = sem("xg_ready")
        x_ready = sem("x_ready")

        tb = table[:, :]

        def par(c):
            return table[:, bass.ds(c, 1)]

        def slot(u):
            return u % RING

        block = ctx.enter_context(nc.Block())

        @block.sync
        def _(sp):
            def cols(w, c):
                return w.rearrange("(k p) n -> p k n", p=P)[:, :, bass.ds(c * P, P)]

            def rows_of(w, k):
                return w[bass.ds(k * P, P), :]

            def load(u0, i, j, src, shaped=True):
                u = u0 + RING * i + j
                dst = w_raw[:, slot(u0 + j), :]
                if shaped:
                    dst = dst.rearrange("p (k n) -> p k n", k=src.shape[1])
                if not (isinstance(u, int) and u < RING):
                    sp.wait_ge(split_ready, u - RING + 1)
                sp.dma_start(dst, src).then_inc(raw_loaded[slot(u0 + j)], 16)

            for s in range(ST):
                sp.dma_start(x[:, s, :], x_in[0, s * P:(s + 1) * P, :]).then_inc(x_loaded[s], 16)
            for j in range(4):
                load(U_POOLIN, 0, j, cols(even_w_in[0], 3 * AC + j))
            fw = [ffn_conv_w[l].rearrange("t (c p) -> (t c) p", p=P) for l in range(DEPTH)]
            fb = [ffn_conv_b[l].rearrange("(c p) -> c p", p=P) for l in range(DEPTH)]
            for l in range(DEPTH):
                sp.dma_start(rows[0:2 * NF, 2 * l, :], fw[l][0:2 * NF, :]).then_inc(rows_loaded, 16)
                sp.dma_start(rows[0:NF, 2 * l + 1, :], fw[l][2 * NF:3 * NF, :]).then_inc(rows_loaded, 16)
                sp.dma_start(rows[NF:2 * NF, 2 * l + 1, :], fb[l]).then_inc(rows_loaded, 16)
            at = 0
            for src in (even_b_pool[0].rearrange("(c p) -> c p", p=P),
                        even_pool_scale[0].rearrange("(c p) -> c p", p=P),
                        odd_conv_w[0].rearrange("t (c p) -> (t c) p", p=P),
                        odd_conv_b[0].rearrange("(c p) -> c p", p=P)):
                n = src.shape[0]
                sp.dma_start(rows[at:at + n, 4, :], src).then_inc(rows_loaded, 16)
                at += n
            sp.dma_start(wpool[:, :, :], even_w_pool[0].rearrange("(g p) n -> p g n", p=P)).then_inc(wpool_loaded, 16)

            def load_ln(n, g, b):
                if n:
                    sp.wait_ge(x_ready, ST * n)
                sp.dma_start(gb[:, 0, :], g.rearrange("(a n) -> a n", a=1).to_broadcast([P, D])).then_inc(gb_loaded, 16)
                sp.dma_start(gb[:, 1, :], b.rearrange("(a n) -> a n", a=1).to_broadcast([P, D])).then_inc(gb_loaded, 16)

            with sp.Fori(0, 2 * AC // RING) as i:
                for j in range(RING):
                    load(U_Q, i, j, cols(even_w_in[0], RING * i + j))
            for j in range(4):
                load(U_V, 0, j, even_w_in[0, 2 * j * P:2 * (j + 1) * P, 2 * ATT:3 * ATT].rearrange(
                    "(k p) n -> p k n", p=P))
            load_ln(0, mix_ln_g[0], mix_ln_b[0])
            for i in range(2):
                for j in range(RING):
                    load(U_OUT0, i, j, rows_of(even_w_out[0], (4, 5, 6, 7, 0, 1, 2, 3)[RING * i + j]), False)

            def ffn(l, u_up, u_down, n):
                with sp.Fori(0, FC // 2) as i:
                    for j in range(RING):
                        load(u_up, i, j, cols(ffn_w_up[l], 2 * i + j // 2 + FC * (j % 2)))
                load_ln(n, ffn_ln_g[l], ffn_ln_b[l])
                with sp.Fori(0, FC // RING) as i:
                    for j in range(RING):
                        load(u_down, i, j, rows_of(ffn_w_down[l], RING * i + j), False)
                for j in range(FC % RING):
                    load(u_down, FC // RING, j, rows_of(ffn_w_down[l], FC - FC % RING + j), False)

            ffn(0, U_UP0, U_DOWN0, 1)
            with sp.Fori(0, DC // 2) as i:
                for j in range(RING):
                    load(U_CH, i, j, cols(odd_w_in[0], DC * (1 + j % 2) + 2 * i + j // 2))
            with sp.Fori(0, DC // RING) as i:
                for j in range(RING):
                    load(U_B, i, j, cols(odd_w_in[0], RING * i + j))
            load_ln(2, mix_ln_g[1], mix_ln_b[1])
            with sp.Fori(0, DC // RING) as i:
                for j in range(RING):
                    load(U_OUT1, i, j, rows_of(odd_w_out[0], RING * i + j), False)
            ffn(1, U_UP1, U_DOWN1, 3)
            for s in range(ST):
                sp.wait_ge(x_ready, 3 * ST + s + 1)
                sp.dma_start(out[0, s * P:(s + 1) * P, :], x[:, s, :]).then_inc(out_stored, 16)
            sp.wait_ge(out_stored, 16 * ST)

        @block.gpsimd
        def _(pool):
            pool.memset(ident[:, :], 0.0).then_inc(const_set, 1)
            pool.memset(ident_b[:, :], 0.0).then_inc(const_set, 1)
            pool.memset(mask_b[:, :], 0.0).then_inc(const_set, 1)
            pool.wait_ge(const_set, 3)
            for m in (ident, ident_b):
                pool.affine_select(out=m[:, :], in_=m[:, :], compare_op=ALU.not_equal, fill=1.0, base=0,
                                   pattern=[[-1, P]], channel_multiplier=1).then_inc(const_ready, 1)
            pool.affine_select(out=mask_b[:, :], in_=mask_b[:, :], compare_op=ALU.is_ge, fill=NEG, base=0,
                               pattern=[[-1, P]], channel_multiplier=1).then_inc(const_ready, 1)
            pool.memset(pool_buf[:, :, :], 0.0).then_inc(const_ready, 1)
            pool.memset(q_pad[:, :, :], 0.0).then_inc(const_ready, 1)
            pool.memset(neg_half[:, :], -0.5).then_inc(const_ready, 1)
            pool.iota(inv_count[:, :], pattern=[[1, 16]], base=1, channel_multiplier=0,
                      allow_small_or_imprecise_dtypes=True).then_inc(const_ready, 1)

            def low(u0, i, j):
                u = u0 + RING * i + j
                pool.wait_ge(hi_ready, u + 1)
                sl = slot(u0 + j)
                pool.tensor_tensor(w_lo[:, sl, :], w_raw[:, sl, :], w_hi[:, sl, :].bitcast(F32),
                                   ALU.subtract).then_inc(split_ready, 1)

            def lows(u0, n):
                if n >= 2 * RING:
                    with pool.Fori(0, n // RING) as i:
                        for j in range(RING):
                            low(u0, i, j)
                    u0, n = u0 + n // RING * RING, n % RING
                for j in range(n):
                    low(u0, 0, j)

            def inv_std(n, s):
                k = ST * n + s + 1
                pool.wait_ge(sq_ready, k)
                pool.tensor_scalar(var[:, s:s + 1], vsum[:, s:s + 1], 1.0 / D, EPS,
                                   ALU.mult, ALU.add).then_inc(var_ready, 1)
                pool.wait_ge(var_ready, k)
                pool.tensor_tensor(rstd[:, s:s + 1], var[:, s:s + 1], neg_half[:, :],
                                   ALU.pow).then_inc(rstd_ready, 1)

            def norm_tail(n, u_next):
                for s in range(ST - 1):
                    inv_std(n, s)
                if u_next < UNITS:
                    low(u_next, 0, 0)
                    low(u_next, 0, 1)
                inv_std(n, ST - 1)
                if u_next < UNITS:
                    low(u_next, 0, 2)
                    low(u_next, 0, 3)

            lows(0, U_UP0)
            norm_tail(0, U_UP0)
            lows(U_UP0 + RING, U_CH - U_UP0 - RING)
            norm_tail(1, U_CH)
            lows(U_CH + RING, U_UP1 - U_CH - RING)
            norm_tail(2, U_UP1)
            lows(U_UP1 + RING, UNITS - U_UP1 - RING)
            norm_tail(3, UNITS)

        def h_at(k):
            return h[:, k, :] if isinstance(k, int) else h[:, bass.ds(k, 1), :].rearrange("p a n -> p (a n)")

        def high(act, u0, i, j):
            u = u0 + RING * i + j
            sl = slot(u0 + j)
            act.wait_ge(raw_loaded[sl], 16 * ((u0 + j) // RING + i) + 16)
            if not (isinstance(u, int) and u < RING):
                act.wait_ge(unit_done, u - RING + 1)
            act.activation(w_hi[:, sl, :], w_raw[:, sl, :], ACT.Copy).then_inc(hi_ready, 1)

        TILES = [(e, c) for e in range(2) for c in range(ST)]

        def p_off(c):
            return P * (c * (c + 1) // 2)

        @block.scalar
        def _(act):
            def xt_high(k, s):
                act.wait_ge(xt_ps, k + 1)
                act.activation(xt_hi[:, :, s * P:(s + 1) * P],
                               ps[:, 2 * s:2 * s + 2, :].rearrange("p a (b n) -> p (a b) n", n=P),
                               ACT.Copy).then_inc(xt_hi_ready, 1)

            def norm_square(n, s):
                k = ST * n + s + 1
                act.wait_ge(mu_ready, k)
                act.activation(conv[:, 0, :, :].rearrange("p a n -> p (a n)"), x[:, s, :], ACT.Square,
                               bias=nmu[:, s:s + 1], accum_out=vsum[:, s:s + 1]).then_inc(sq_ready, 1)

            def norm_tail(n, u_next):
                for s in range(ST):
                    if s == ST - 1 and u_next < UNITS:
                        for j in range(3):
                            high(act, u_next, 0, j)
                    norm_square(n, s)
                    if s and n < 3:
                        xt_high(ST * (n + 1) + s - 1, s - 1)
                if n < 3:
                    high(act, u_next, 0, 3)
                    xt_high(ST * (n + 1) + ST - 1, ST - 1)

            def down(h0, order, u0, nch, n, u_next):
                def post(i, j):
                    high(act, u0 + RING, i, j)
                    jj = RING * i + j + RING
                    act.wait_ge(h_ready, h0 + jj + 1)
                    act.wait_ge(unit_done, u0 + jj - RING + 1)
                    k = order(jj)
                    act.activation(ht_hi[:, j, :], h_at(k), ACT.Copy).then_inc(ht_hi_ready, 1)
                m = nch - TAIL
                if m >= 2 * RING:
                    with act.Fori(0, m // RING) as i:
                        for j in range(RING):
                            post(i, j)
                    for j in range(m % RING):
                        post(m // RING, j)
                else:
                    for j in range(m):
                        post(0, j)
                norm_tail(n, u_next)

            def ht_first(h0, order):
                for j in range(RING):
                    act.wait_ge(h_ready, h0 + j + 1)
                    act.activation(ht_hi[:, j, :], h_at(order(j)), ACT.Copy).then_inc(ht_hi_ready, 1)

            def glu(l, u0, free0, h0):
                wc, bc = col_ffn(l, 2), col_ffn(l, 3)

                def pair(i, q):
                    c = 2 * i + q
                    for e in range(2):
                        high(act, u0 + RING, i, 2 * q + e)
                    act.wait_ge(h_ready, h0 + c - 1)
                    for e in range(2):
                        act.wait_ge(unit_done, u0 + 2 * c + e + 1)
                        act.activation(conv[:, q, e, :], ps[:, 2 * q + e, :], ACT.Identity,
                                       scale=par(c + (wc + e * FC)), bias=par(c + (bc + e * FC))
                                       ).then_inc(conv_base, 1)
                    act.wait_ge(bank_free, free0 + 2 * c + 1)
                    act.activation(act_g[:, q, :], conv[:, q, 0, :], ACT.Silu).then_inc(gate_ready, 1)

                with act.Fori(0, FC // 2 - 1) as i:
                    pair(i, 0)
                    pair(i, 1)
                ht_first(h0, lambda j: j)
                pair(FC // 2 - 1, 0)
                pair(FC // 2 - 1, 1)

            for s in range(ST):
                xt_high(s, s)
            for j in range(RING):
                high(act, 0, 0, j)
            with act.Fori(0, 3) as i:
                for j in range(RING):
                    high(act, RING, i, j)
            act.wait_ge(unit_done, U_OUT0)
            for s in (2, 3):
                act.activation(h[:, SLOT_V + s, :], ps[:, 4 + s, :], ACT.Copy).then_inc(v_ready, 1)
            for j in range(RING):
                high(act, U_OUT0, 0, j)
            ht_first(H_OUT0, lambda j: j + 4)

            def att_pair(p):
                def move(t):
                    e, c = TILES[t]
                    if c in (0, 3):
                        act.wait_ge(pt_done, 8 * p + t + 1)
                        act.activation(probs_t[:, p_off(c):p_off(c + 1)], ps[:, 4 + c % 2, 0:P * (c + 1)],
                                       ACT.Copy).then_inc(pt_act, 1)
                for t, (e, c) in enumerate(TILES):
                    act.wait_ge(max_ready, 8 * p + t + 1)
                    act.activation(probs[:, e, p_off(c):p_off(c + 1)], ps[:, c, 0:P * (c + 1)], ACT.Exp,
                                   bias=neg_max[:, e, c:c + 1],
                                   accum_out=prob_sum[:, e, c:c + 1]).then_inc(probs_ready, 1)
                    if t:
                        move(t - 1)
                move(7)

            with act.Fori(0, AC) as p:
                att_pair(p)

            down(H_OUT0, lambda j: (j + 4) % 8, U_OUT0, DC, 0, U_UP0)
            glu(0, U_UP0, FREE_UP0, H_DOWN0)
            down(H_DOWN0, lambda j: j, U_DOWN0, FC, 1, U_CH)

            with act.Fori(0, DC // 2) as i:
                for q in range(2):
                    c = 2 * i + q
                    for e in range(2):
                        high(act, U_CH + RING, i, 2 * q + e)
                    act.wait_ge(unit_done, U_CH + 2 * c + 1)
                    act.wait_ge(bank_free, FREE_CH + 2 * c - 2)
                    act.activation(conv[:, q, 0, :], ps[:, 2 * q, :], ACT.Copy).then_inc(c_ready, 1)
                    act.wait_ge(bank_free, FREE_CH + 2 * c + 2)
                    act.activation(h_at(c), conv[:, q, 1, :], ACT.Identity, scale=par(c + (COL_ODDW + 2 * DC)),
                                   bias=par(c + COL_ODDB)).then_inc(conv_base, 1)
            for j in range(RING):
                high(act, U_B + RING, 0, j)
            ht_first(H_OUT1, lambda j: j)
            for j in range(RING):
                high(act, U_OUT1, 0, j)
            down(H_OUT1, lambda j: j, U_OUT1, DC, 2, U_UP1)
            glu(1, U_UP1, FREE_UP1, H_DOWN1)
            down(H_DOWN1, lambda j: j, U_DOWN1, FC, 3, UNITS)

        @block.vector
        def _(dve):
            def h_part(k, a, b):
                return h[:, bass.ds(k, 1), a:b].rearrange("p a n -> p (a n)")

            def xt_low(k, s):
                dve.wait_ge(xt_hi_ready, k + 1)
                sl = slice(s * P, (s + 1) * P)
                dve.tensor_tensor(xt_lo[:, :, sl],
                                  ps[:, 2 * s:2 * s + 2, :].rearrange("p a (b n) -> p (a b) n", n=P),
                                  xt_hi[:, :, sl].bitcast(F32), ALU.subtract).then_inc(xt_ready, 1)

            def ht_low(h0, order, j, sl):
                dve.wait_ge(ht_hi_ready, h0 + j + 1)
                dve.tensor_tensor(ht_lo[:, sl, :], h_at(order(j)), ht_hi[:, sl, :].bitcast(F32),
                                  ALU.subtract).then_inc(ht_ready, 1)

            def ht_first(h0, order):
                for j in range(RING):
                    ht_low(h0, order, j, j)

            def norm_start(n, s, u_end):
                k = ST * n + s + 1
                if s < ST - 1:
                    dve.wait_ge(tile_done, (ST - 1) * n + s + 1)
                else:
                    dve.wait_ge(unit_done, u_end)
                xs = x[:, s, :].rearrange("p (a n) -> p a n", a=2)
                dve.scalar_tensor_tensor(xs, xs, ALPHA, ps[:, 2 * s:2 * s + 2, :], ALU.mult, ALU.add,
                                         accum_out=zsum[:, s:s + 1]).then_inc(z_ready, 1)
                dve.wait_ge(z_ready, k)
                dve.tensor_scalar(nmu[:, s:s + 1], zsum[:, s:s + 1], -1.0 / D, None,
                                  ALU.mult).then_inc(mu_ready, 1)

            def norm_gain(n, s):
                k = ST * n + s + 1
                dve.wait_ge(mu_ready, k)
                dve.wait_ge(sq_ready, k)
                dve.scalar_tensor_tensor(x[:, s, :], x[:, s, :], nmu[:, s:s + 1], gb[:, 0, :],
                                         ALU.add, ALU.mult).then_inc(xg_ready, 1)

            def norm_end(n, s):
                k = ST * n + s + 1
                dve.wait_ge(xg_ready, k)
                dve.wait_ge(rstd_ready, k)
                dve.scalar_tensor_tensor(x[:, s, :], x[:, s, :], rstd[:, s:s + 1], gb[:, 1, :],
                                         ALU.mult, ALU.add).then_inc(x_ready, 1)

            def down(h0, order, u0, nch, n):
                m = nch - TAIL
                if m >= 2 * RING:
                    with dve.Fori(0, m // RING) as i:
                        for j in range(RING):
                            ht_low(h0, order, RING * i + (j + RING), j)
                    for j in range(m % RING):
                        ht_low(h0, order, m // RING * RING + j + RING, j)
                else:
                    for j in range(m):
                        ht_low(h0, order, j + RING, j)
                dve.wait_ge(gb_loaded, 32 * (n + 1))
                for s in range(ST):
                    norm_start(n, s, u0 + nch)
                    if s and n < 3 and s < ST - 1:
                        xt_low(ST * (n + 1) + s - 1, s - 1)
                    norm_gain(n, s)
                    norm_end(n, s)
                if n < 3:
                    for s in (ST - 2, ST - 1):
                        xt_low(ST * (n + 1) + s, s)

            def glu(l, conv0, free0, h0):
                def pair(i, q):
                    c = 2 * i + q
                    for e in range(2):
                        dve.wait_ge(conv_base, conv0 + 2 * c + e + 1)
                        dve.scalar_tensor_tensor(conv[:, q, e, 1:SEQ], ps[:, 2 * q + e, 0:SEQ - 1],
                                                 par(c + (col_ffn(l, 1) + e * FC)), conv[:, q, e, 1:SEQ],
                                                 ALU.mult, ALU.add).then_inc(tap1, 1)
                    for e in range(2):
                        dve.wait_ge(tap1, conv0 + 2 * c + e + 1)
                        dve.scalar_tensor_tensor(conv[:, q, e, 2:SEQ], ps[:, 2 * q + e, 0:SEQ - 2],
                                                 par(c + (col_ffn(l, 0) + e * FC)), conv[:, q, e, 2:SEQ],
                                                 ALU.mult, ALU.add).then_inc(bank_free, 1)
                    dve.wait_ge(bank_free, free0 + 2 * c + 2)
                    dve.wait_ge(gate_ready, FC * l + c + 1)
                    dve.tensor_tensor(h_at(c), act_g[:, q, :], conv[:, q, 1, :],
                                      ALU.mult).then_inc(h_ready, 1)

                with dve.Fori(0, FC // 2 - 1) as i:
                    pair(i, 0)
                    pair(i, 1)
                ht_first(h0, lambda j: j)
                pair(FC // 2 - 1, 0)
                pair(FC // 2 - 1, 1)

            dve.wait_ge(const_ready, 7)
            dve.reciprocal(inv_count[:, :], inv_count[:, :]).then_inc(inv_ready, 1)
            for s in range(ST):
                xt_low(s, s)
            dve.wait_ge(table_t, 1)
            dve.tensor_copy(table[:, :], ps[:, 4, 0:COLS]).then_inc(table_ready, 1)
            dve.wait_ge(inv_ready, 1)

            steps = 0
            for g in range(GROUPS):
                win = 2 << g
                here = slice(PAD, PAD + SEQ)
                u_buf = pool_buf[:, 0, here]
                dve.wait_ge(unit_done, U_POOLIN + g + 1)
                dve.tensor_copy(u_buf, ps[:, g, :]).then_inc(bank_free, 1)
                dve.wait_ge(bank_free, g + 1)
                src = 0
                for i in range(g + 1):
                    dst = 1 + i % 2
                    dve.tensor_tensor(pool_buf[:, dst, here], pool_buf[:, src, here],
                                      pool_buf[:, src, PAD - (1 << i):PAD + SEQ - (1 << i)],
                                      ALU.add).then_inc(pool_step, 1)
                    steps += 1
                    dve.wait_ge(pool_step, steps)
                    src = dst
                dve.scalar_tensor_tensor(pooled[:, g, :], pool_buf[:, src, here], 1.0 / win, u_buf,
                                         ALU.mult, ALU.subtract).then_inc(pool_step, 1)
                n = win - 1
                dve.tensor_tensor(pool_buf[:, 3 - src, PAD:PAD + n], pool_buf[:, src, PAD:PAD + n],
                                  inv_count[:, 0:n], ALU.mult).then_inc(pool_step, 1)
                steps += 2
                dve.wait_ge(pool_step, steps)
                dve.tensor_tensor(pooled[:, g, 0:n], pool_buf[:, 3 - src, PAD:PAD + n],
                                  pool_buf[:, 0, PAD:PAD + n], ALU.subtract).then_inc(pooled_ready, 1)
                dve.wait_ge(pooled_ready, g + 1)

            for j in range(AC):
                dve.wait_ge(unit_done, U_Q + j + 1)
                dve.tensor_scalar(h[:, SLOT_Q + j, :], ps[:, j, :], SCALE, None, ALU.mult).then_inc(bank_free, 1)
            for j in range(AC):
                dve.wait_ge(unit_done, U_K + j + 1)
                dve.tensor_copy(h[:, SLOT_K + j, :], ps[:, j, :]).then_inc(bank_free, 1)

            def stage_q(p, e):
                half = slice(HEAD_DIM * e, HEAD_DIM * (e + 1))
                src = h[half, bass.ds(p + SLOT_Q, 1), :].rearrange("p a n -> p (a n)")
                dve.tensor_copy(q_pad[half, e, :], src).then_inc(q_staged, 1)

            dve.wait_ge(bank_free, 8)
            stage_q(0, 0)
            stage_q(0, 1)
            dve.wait_ge(unit_done, U_OUT0)
            for s in (0, 1):
                dve.tensor_copy(h[:, SLOT_V + s, :], ps[:, 4 + s, :]).then_inc(v_dve, 1)
            dve.wait_ge(table_ready, 1)
            for g in range(GROUPS):
                dve.wait_ge(mixed_done, g + 1)
                dve.tensor_scalar(h[:, 4 + g, :], ps[:, g, :], table[:, COL_BPOOL + g:COL_BPOOL + g + 1],
                                  table[:, COL_PSCALE + g:COL_PSCALE + g + 1],
                                  ALU.add, ALU.mult).then_inc(h_ready, 1)
            ht_first(H_OUT0, lambda j: j + 4)

            def att_pair(p, more):
                def move(t):
                    e, c = TILES[t]
                    if c in (1, 2):
                        dve.wait_ge(pt_done, 8 * p + t + 1)
                        dve.tensor_copy(probs_t[:, p_off(c):p_off(c + 1)],
                                        ps[:, 4 + c % 2, 0:P * (c + 1)]).then_inc(pt_dve, 1)

                def head_out(e):
                    dve.wait_ge(probs_ready, 8 * p + 4 * e + 4)
                    dve.reciprocal(prob_inv[:, e, :], prob_sum[:, e, :]).then_inc(inv_sum, 1)
                    dve.wait_ge(inv_sum, 2 * p + e + 1)
                    dve.wait_ge(o_done, 2 * p + e + 1)
                    dst = o_nat[:, :, bass.ds(P * p + HEAD_DIM * e, HEAD_DIM)]
                    dve.tensor_tensor(dst, ps[:, 6 + e, 0:ST * HEAD_DIM].rearrange("p (c n) -> p c n", c=ST),
                                      prob_inv[:, e, :].unsqueeze(2).to_broadcast([P, ST, HEAD_DIM]),
                                      ALU.mult).then_inc(o_ready, 1)

                for t, (e, c) in enumerate(TILES):
                    dve.wait_ge(scores_done, 8 * p + t + 1)
                    dve.reduce_max(neg_max[:, e, c:c + 1], ps[:, c, 0:P * (c + 1)], AX_X,
                                   negate=True).then_inc(max_ready, 1)
                    if t:
                        move(t - 1)
                    if t == 4 and more:
                        stage_q(p + 1, 0)
                    if t == 6:
                        head_out(0)
                move(7)
                if more:
                    stage_q(p + 1, 1)
                head_out(1)

            with dve.Fori(0, AC - 1) as p:
                att_pair(p, True)
            att_pair(AC - 1, False)
            for j in range(AC):
                dve.wait_ge(ot_done, j + 1)
                dve.tensor_copy(h[:, j, :], ps[:, j, :]).then_inc(h_ready, 1)

            down(H_OUT0, lambda j: (j + 4) % 8, U_OUT0, DC, 0)
            glu(0, CONV_UP0, FREE_UP0, H_DOWN0)
            down(H_DOWN0, lambda j: j, U_DOWN0, FC, 1)

            with dve.Fori(0, DC // 2) as i:
                for q in range(2):
                    c = 2 * i + q
                    dve.wait_ge(c_ready, c + 1)
                    dve.wait_ge(unit_done, U_CH + 2 * c + 2)
                    dve.tensor_tensor(conv[:, q, 1, :], ps[:, 2 * q + 1, :], conv[:, q, 0, :],
                                      ALU.mult).then_inc(bank_free, 2)
                    dve.wait_ge(conv_base, CONV_CH + c + 1)
                    dve.scalar_tensor_tensor(h_part(c, 1, SEQ), conv[:, q, 1, 0:SEQ - 1],
                                             par(c + (COL_ODDW + DC)), h_part(c, 1, SEQ),
                                             ALU.mult, ALU.add).then_inc(tap1, 1)
                    dve.wait_ge(tap1, CONV_CH + c + 1)
                    dve.scalar_tensor_tensor(h_part(c, 2, SEQ), conv[:, q, 1, 0:SEQ - 2],
                                             par(c + COL_ODDW), h_part(c, 2, SEQ),
                                             ALU.mult, ALU.add).then_inc(short_ready, 1)
            dve.wait_ge(short_ready, DC)
            for j in range(DC):
                if j == RING:
                    ht_first(H_OUT1, lambda j: j)
                dve.wait_ge(unit_done, U_B + j + 1)
                dve.tensor_tensor(h[:, j, :], ps[:, j % RING, :], h[:, j, :], ALU.mult).then_inc(h_ready, 1)
            down(H_OUT1, lambda j: j, U_OUT1, DC, 2)
            glu(1, CONV_UP1, FREE_UP1, H_DOWN1)
            down(H_DOWN1, lambda j: j, U_DOWN1, FC, 3)

        @block.tensor
        def _(pe):
            def three(dst, a_hi, a_lo, b_hi, b_lo, start, stop):
                pe.matmul(dst, a_hi, b_hi, start=start, stop=False)
                pe.matmul(dst, a_hi, b_lo, start=False, stop=False)
                return pe.matmul(dst, a_lo, b_hi, start=False, stop=stop)

            def x_transpose(s):
                for d in range(DC):
                    last = pe.transpose(ps[:, 2 * s + d // 4, (d % 4) * P:(d % 4 + 1) * P],
                                        x[:, s, d * P:(d + 1) * P], ident[:, :])
                last.then_inc(xt_ps, 1)

            def up_unit(u0, i, j, bank):
                pe.wait_ge(split_ready, u0 + RING * i + (j + 1))
                sl = slot(u0 + j)
                for k in range(DC):
                    ks = slice(k * P, (k + 1) * P)
                    last = three(ps[:, bank, :], w_hi[:, sl, ks], w_lo[:, sl, ks],
                                 xt_hi[:, k, :], xt_lo[:, k, :], k == 0, k == DC - 1)
                last.then_inc(unit_done, 1)

            def down_part(sl, j, s, start, stop):
                ss = slice(s * P, (s + 1) * P)
                for n in range(2):
                    ns = slice(n * 512, (n + 1) * 512)
                    last = three(ps[:, 2 * s + n, :], ht_hi[:, j, ss], ht_lo[:, j, ss],
                                 w_hi[:, sl, ns], w_lo[:, sl, ns], start, stop)
                return last

            def down(h0, u0, nch, n, banks_read):
                def unit(i, j, first=False):
                    u = u0 + RING * i + j
                    pe.wait_ge(split_ready, u + 1)
                    pe.wait_ge(ht_ready, h0 + RING * i + (j + 1))
                    for s in (2, 3, 0, 1):
                        if first and s == 0:
                            pe.wait_ge(*banks_read)
                        last = down_part(slot(u0 + j), j, s, first, False)
                    last.then_inc(unit_done, 1)

                m = nch - TAIL
                for j in range(RING):
                    unit(0, j, j == 0)
                if m >= 2 * RING:
                    with pe.Fori(1, m // RING) as i:
                        for j in range(RING):
                            unit(i, j)
                    for j in range(m % RING):
                        unit(m // RING, j)
                pe.wait_ge(split_ready, u0 + nch)
                pe.wait_ge(ht_ready, h0 + nch)
                for s in range(ST):
                    for j in range(m, nch):
                        last = down_part(slot(u0 + j), j % RING, s, False, j == nch - 1)
                        if s == ST - 1:
                            last.then_inc(unit_done, 1)
                    if s < ST - 1:
                        last.then_inc(tile_done, 1)
                    if s and n < 3:
                        pe.wait_ge(x_ready, ST * n + s)
                        x_transpose(s - 1)
                if n < 3:
                    pe.wait_ge(x_ready, ST * (n + 1))
                    x_transpose(ST - 1)
                    pe.wait_ge(xt_ready, ST * (n + 2))

            def glu(u0, free0):
                with pe.Fori(0, FC // 2) as i:
                    for j in range(RING):
                        pe.wait_ge(bank_free, RING * i + (free0 + j + 1 - RING))
                        up_unit(u0, i, j, j)

            pe.wait_ge(const_ready, 3)
            for s in range(ST):
                pe.wait_ge(x_loaded[s], 16)
                x_transpose(s)
            pe.wait_ge(rows_loaded, 16 * (3 * DEPTH + 4))
            pe.wait_ge(xt_ready, ST)
            for r in range(5):
                n, at = (2 * NF, 2 * NF * r) if r < 4 else (COLS - COL_BPOOL, COL_BPOOL)
                last = pe.transpose(ps[:, 4, at:at + n], rows[0:n, r, :], ident[0:n, 0:n])
            last.then_inc(table_t, 1)

            for j in range(4):
                up_unit(U_POOLIN, 0, j, j)
            with pe.Fori(0, 2) as i:
                for j in range(RING):
                    pe.wait_ge(bank_free, RING * i + j + 1)
                    up_unit(U_Q, i, j, j)
            pe.wait_ge(table_ready, 1)
            for j in range(4):
                pe.wait_ge(split_ready, U_V + j + 1)
                for s in range(ST):
                    ss = slice(s * P, (s + 1) * P)
                    for kk in range(2):
                        ns = slice(kk * ATT, (kk + 1) * ATT)
                        k = 2 * j + kk
                        last = three(ps[:, 4 + s, :], xt_hi[:, k, ss], xt_lo[:, k, ss],
                                     w_hi[:, j, ns], w_lo[:, j, ns], k == 0, k == DC - 1)
                last.then_inc(unit_done, 1)
            pe.wait_ge(wpool_loaded, 16)
            pe.wait_ge(bank_free, 12)
            for g in range(GROUPS):
                pe.wait_ge(pooled_ready, g + 1)
                pe.matmul(ps[:, g, :], wpool[:, g, :], pooled[:, g, :], start=True, stop=True
                          ).then_inc(mixed_done, 1)

            def scores(p, t):
                e, c = TILES[t]
                width = P * (c + 1)
                pe.matmul(ps[:, c, 0:width], q_pad[:, e, c * P:(c + 1) * P],
                          h[:, bass.ds(p + SLOT_K, 1), 0:width].rearrange("p a n -> p (a n)"),
                          start=True, stop=False)
                pe.matmul(ps[:, c, c * P:width], ident_b[:, :], mask_b[:, :],
                          start=False, stop=True).then_inc(scores_done, 1)

            def transposed(p, t):
                e, c = TILES[t]
                pe.wait_ge(probs_ready, 8 * p + t + 1)
                for kc in range(c + 1):
                    last = pe.transpose(ps[:, 4 + c % 2, kc * P:(kc + 1) * P],
                                        probs[:, e, p_off(c) + kc * P:p_off(c) + (kc + 1) * P], ident[:, :])
                last.then_inc(pt_done, 1)

            def outputs(p, t):
                e, c = TILES[t]
                if c in (0, 3):
                    pe.wait_ge(pt_act, 4 * p + 2 * e + (1 if c == 0 else 2))
                else:
                    pe.wait_ge(pt_dve, 4 * p + 2 * e + c)
                for kc in range(c + 1):
                    at = p_off(c) + kc * P
                    last = pe.matmul(ps[:, 6 + e, c * HEAD_DIM:(c + 1) * HEAD_DIM], probs_t[:, at:at + P],
                                     h[:, SLOT_V + kc, bass.ds(P * p + HEAD_DIM * e, HEAD_DIM)],
                                     start=(kc == 0), stop=(kc == c))
                if c == ST - 1:
                    last.then_inc(o_done, 1)

            def att_pair(p, more):
                for t in range(8):
                    if t == 1:
                        pe.wait_ge(q_staged, 2 * p + 2)
                    if t + 3 < 8:
                        scores(p, t + 3)
                    elif more:
                        if t == 5:
                            pe.wait_ge(q_staged, 2 * p + 3)
                        scores(p + 1, t + 3 - 8)
                    transposed(p, t)
                    if t:
                        outputs(p, t - 1)
                outputs(p, 7)

            pe.wait_ge(h_ready, 4)
            pe.wait_ge(q_staged, 1)
            pe.wait_ge(v_ready, 2)
            pe.wait_ge(v_dve, 2)
            for t in range(3):
                scores(0, t)
            with pe.Fori(0, AC - 1) as p:
                att_pair(p, True)
            att_pair(AC - 1, False)
            pe.wait_ge(o_ready, 2 * AC)
            for j in range(AC):
                for s in range(ST):
                    last = pe.transpose(ps[:, j, s * P:(s + 1) * P], o_nat[:, s, j * P:(j + 1) * P], ident[:, :])
                last.then_inc(ot_done, 1)

            down(H_OUT0, U_OUT0, DC, 0, (h_ready, H_DOWN0))
            glu(U_UP0, FREE_UP0)
            down(H_DOWN0, U_DOWN0, FC, 1, (bank_free, FREE_CH))
            with pe.Fori(0, DC // 2) as i:
                for j in range(RING):
                    pe.wait_ge(bank_free, RING * i + (FREE_CH + 2 * (j // 2) - 2))
                    up_unit(U_CH, i, j, j)
            for j in range(DC):
                if j < RING:
                    pe.wait_ge(bank_free, FREE_UP1)
                else:
                    pe.wait_ge(h_ready, H_OUT1 + j - RING + 1)
                up_unit(U_B, 0, j, j % RING)
            down(H_OUT1, U_OUT1, DC, 2, (h_ready, H_DOWN1))
            glu(U_UP1, FREE_UP1)
            down(H_DOWN1, U_DOWN1, FC, 3, (bank_free, FREE_END))


_INS = ["x", "even_w_in", "even_w_pool", "even_b_pool", "even_pool_scale", "even_w_out",
        "odd_w_in", "odd_conv_w", "odd_conv_b", "odd_w_out", "mix_ln_g", "mix_ln_b",
        "ffn_w_up", "ffn_conv_w", "ffn_conv_b", "ffn_w_down", "ffn_ln_g", "ffn_ln_b"]


def kernel(**inputs):
    import numpy as _np
    import concourse.bacc as _bacc
    from concourse import mybir as _mybir
    from concourse.bass_utils import run_bass_kernel_spmd as _run

    nc = _bacc.Bacc("TRN2", target_bir_lowering=False, num_devices=1)
    arrays, args = {}, []
    for name in _INS:
        a = _np.ascontiguousarray(inputs[name])
        arrays[f"in_{name}"] = a
        args.append(nc.dram_tensor(f"in_{name}", a.shape, _mybir.dt.from_np(a.dtype), kind="ExternalInput").ap())
    out = nc.dram_tensor("out_x", inputs["x"].shape, _mybir.dt.float32, kind="ExternalOutput").ap()
    trunk_program(nc, *args, out)
    return _run(nc, [arrays], core_ids=[0]).results[0]["out_x"]
```

```python
from contextlib import ExitStack

import concourse.bass as bass
from concourse import mybir

ALU = mybir.AluOpType
ACT = mybir.ActivationFunctionType
F32 = mybir.dt.float32
F32R = mybir.dt.float32r
BF16 = mybir.dt.bfloat16
AX_X = mybir.AxisListType.X
P = 128


def trunk_program(nc, x_in, even_w_in, even_w_pool, even_b_pool, even_pool_scale, even_w_out,
                  odd_w_in, odd_conv_w, odd_conv_b, odd_w_out, mix_ln_g, mix_ln_b,
                  ffn_w_up, ffn_conv_w, ffn_conv_b, ffn_w_down, ffn_ln_g, ffn_ln_b, out):
    _, SEQ, D = x_in.shape
    DEPTH = mix_ln_g.shape[0]
    DFF = ffn_w_down.shape[1]
    ATT = D // 2
    HEAD_DIM = 64
    ST = SEQ // P
    DC = D // P
    FC = DFF // P
    AC = ATT // P
    GROUPS = AC
    ALPHA = float((2 * DEPTH) ** 0.25)
    EPS = 1e-5
    NEG = -1e30
    SCALE = float(HEAD_DIM) ** -0.5
    RING = 4
    TAIL = 4
    PAD = 8
    ACC = 4 + 4
    assert (SEQ, D, DEPTH, FC % 2) == (512, 1024, 2, 0)

    U_POOLIN, U_V, U_Q, U_K = 0, 4, 8, 12
    U_OUT0 = 16
    U_UP0 = U_OUT0 + DC
    U_DOWN0 = U_UP0 + 2 * FC
    U_CH = U_DOWN0 + FC
    U_B = U_CH + 2 * DC
    U_OUT1 = U_B + DC
    U_UP1 = U_OUT1 + DC
    U_DOWN1 = U_UP1 + 2 * FC
    UNITS = U_DOWN1 + FC

    FREE_UP0 = 12
    FREE_CH = FREE_UP0 + 2 * FC
    FREE_UP1 = FREE_CH + 2 * DC
    FREE_END = FREE_UP1 + 2 * FC
    H_OUT0 = 0
    H_DOWN0 = H_OUT0 + DC
    H_OUT1 = H_DOWN0 + FC
    H_DOWN1 = H_OUT1 + DC
    CONV_UP0, CONV_CH, CONV_UP1 = 0, 2 * FC, 2 * FC + DC

    SLOT_O, SLOT_Q, SLOT_V = DC, DC + AC, DC + 2 * AC

    NF = 2 * FC

    def col_ffn(layer, tap):
        return (layer * 4 + tap) * NF
    COL_BPOOL = DEPTH * 4 * NF
    COL_PSCALE = COL_BPOOL + GROUPS
    COL_ODDW = COL_PSCALE + GROUPS
    COL_ODDB = COL_ODDW + 3 * DC
    COLS = COL_ODDB + DC

    with ExitStack() as ctx:
        def sb(name, shape, dt=F32):
            return ctx.enter_context(nc.sbuf_tensor(name, shape, dt))

        def sem(name):
            return ctx.enter_context(nc.semaphore(name))

        ps = ctx.enter_context(nc.psum_tensor("ps", [P, ACC, 512], F32))

        w_raw = sb("w_raw", [P, RING, D])
        w_hi = sb("w_hi", [P, RING, D], F32R)
        w_lo = sb("w_lo", [P, RING, D], F32R)
        xt_hi = sb("xt_hi", [P, DC, SEQ], F32R)
        xt_lo = sb("xt_lo", [P, DC, SEQ], F32R)
        x = sb("x", [P, ST, D])
        h = sb("h", [P, FC, SEQ])
        ht_hi = sb("ht_hi", [P, RING, SEQ], F32R)
        ht_lo = sb("ht_lo", [P, RING, SEQ], F32R)
        gb = sb("gb", [P, 2, D])
        conv = sb("conv", [P, 2, 2, SEQ])
        act_g = sb("act_g", [P, 2, SEQ])
        probs = sb("probs", [P, 2, 1280])
        probs_t = sb("probs_t", [P, 1280])
        q_hi = sb("q_hi", [P, 2, SEQ], F32R)
        q_lo = sb("q_lo", [P, 2, SEQ], F32R)
        wpool = sb("wpool", [P, GROUPS, P])
        table = sb("table", [P, COLS])
        ident = sb("ident", [P, P])
        ident_b = sb("ident_b", [P, P], BF16)
        mask_b = sb("mask_b", [P, P], BF16)
        inv_count = sb("inv_count", [P, 16])
        stats = sb("stats", [P, 6, ST])
        neg_half = sb("neg_half", [P, 1])
        att_stat = sb("att_stat", [P, 3, 2, ST])

        pool_buf = probs[:, :, :].rearrange("p a b -> p (a b)")[:, 0:3 * (PAD + SEQ)].rearrange(
            "p (a b) -> p a b", a=3)
        rows = probs[:, :, :].rearrange("p a b -> p (a b)")[:, 3 * (PAD + SEQ):3 * (PAD + SEQ) + 5 * P].rearrange(
            "p (a b) -> p a b", a=5)
        xg = act_g[:, :, :].rearrange("p a n -> p (a n)")
        o_nat = h[:, SLOT_O:SLOT_O + ST, :]
        pooled = o_nat
        k_hi, k_lo = ht_hi, ht_lo

        zsum, nmu, vsum, var, rstd = (stats[:, i, :] for i in range(5))
        neg_max, prob_sum, prob_inv = (att_stat[:, i, :, :] for i in range(3))

        raw_loaded = [sem(f"raw_loaded{i}") for i in range(RING)]
        x_loaded = [sem(f"x_loaded{i}") for i in range(ST)]
        rows_loaded = sem("rows_loaded")
        wpool_loaded = sem("wpool_loaded")
        gb_loaded = sem("gb_loaded")
        out_stored = sem("out_stored")
        const_set = sem("const_set")
        const_ready = sem("const_ready")
        inv_ready = sem("inv_ready")
        hi_ready = sem("hi_ready")
        split_ready = sem("split_ready")
        unit_done = sem("unit_done")
        bank_free = sem("bank_free")
        table_t = sem("table_t")
        table_ready = sem("table_ready")
        xt_ps = sem("xt_ps")
        xt_hi_ready = sem("xt_hi_ready")
        xt_ready = sem("xt_ready")
        h_ready = sem("h_ready")
        ht_hi_ready = sem("ht_hi_ready")
        ht_ready = sem("ht_ready")
        pool_step = sem("pool_step")
        pooled_ready = sem("pooled_ready")
        mixed_done = sem("mixed_done")
        v_ready = sem("v_ready")
        v_dve = sem("v_dve")
        q_copied = sem("q_copied")
        q_high = sem("q_high")
        q_staged = sem("q_staged")
        k_high = sem("k_high")
        scores_done = sem("scores_done")
        max_ready = sem("max_ready")
        probs_ready = sem("probs_ready")
        pt_done = sem("pt_done")
        pt_act = sem("pt_act")
        pt_dve = sem("pt_dve")
        o_done = sem("o_done")
        inv_sum = sem("inv_sum")
        o_ready = sem("o_ready")
        ot_done = sem("ot_done")
        conv_base = sem("conv_base")
        tap1 = sem("tap1")
        gate_ready = sem("gate_ready")
        c_ready = sem("c_ready")
        short_ready = sem("short_ready")
        tile_done = sem("tile_done")
        z_ready = sem("z_ready")
        mu_ready = sem("mu_ready")
        sq_ready = sem("sq_ready")
        var_ready = sem("var_ready")
        rstd_ready = sem("rstd_ready")
        xg_ready = sem("xg_ready")
        x_ready = sem("x_ready")

        tb = table[:, :]

        def par(c):
            return table[:, bass.ds(c, 1)]

        def slot(u):
            return u % RING

        block = ctx.enter_context(nc.Block())

        @block.sync
        def _(sp):
            def cols(w, c):
                return w.rearrange("(k p) n -> p k n", p=P)[:, :, bass.ds(c * P, P)]

            def rows_of(w, k):
                return w[bass.ds(k * P, P), :]

            def load(u0, i, j, src, shaped=True):
                u = u0 + RING * i + j
                dst = w_raw[:, slot(u0 + j), :]
                if shaped:
                    dst = dst.rearrange("p (k n) -> p k n", k=src.shape[1])
                if not (isinstance(u, int) and u < RING):
                    sp.wait_ge(split_ready, u - RING + 1)
                sp.dma_start(dst, src).then_inc(raw_loaded[slot(u0 + j)], 16)

            def load_x(s):
                sp.dma_start(x[:, s, :], x_in[0, s * P:(s + 1) * P, :]).then_inc(x_loaded[s], 16)

            load_x(0)
            load_x(1)
            for j in range(4):
                load(U_POOLIN, 0, j, cols(even_w_in[0], 3 * AC + j))
                if j in (1, 2):
                    load_x(j + 1)
            fw = [ffn_conv_w[l].rearrange("t (c p) -> (t c) p", p=P) for l in range(DEPTH)]
            fb = [ffn_conv_b[l].rearrange("(c p) -> c p", p=P) for l in range(DEPTH)]
            for l in range(DEPTH):
                sp.dma_start(rows[0:2 * NF, 2 * l, :], fw[l][0:2 * NF, :]).then_inc(rows_loaded, 16)
                sp.dma_start(rows[0:NF, 2 * l + 1, :], fw[l][2 * NF:3 * NF, :]).then_inc(rows_loaded, 16)
                sp.dma_start(rows[NF:2 * NF, 2 * l + 1, :], fb[l]).then_inc(rows_loaded, 16)
            at = 0
            for src in (even_b_pool[0].rearrange("(c p) -> c p", p=P),
                        even_pool_scale[0].rearrange("(c p) -> c p", p=P),
                        odd_conv_w[0].rearrange("t (c p) -> (t c) p", p=P),
                        odd_conv_b[0].rearrange("(c p) -> c p", p=P)):
                n = src.shape[0]
                sp.dma_start(rows[at:at + n, 4, :], src).then_inc(rows_loaded, 16)
                at += n
            sp.dma_start(wpool[:, :, :], even_w_pool[0].rearrange("(g p) n -> p g n", p=P)).then_inc(wpool_loaded, 16)

            def load_ln(n, g, b):
                if n:
                    sp.wait_ge(x_ready, ST * n)
                sp.dma_start(gb[:, 0, :], g.rearrange("(a n) -> a n", a=1).to_broadcast([P, D])).then_inc(gb_loaded, 16)
                sp.dma_start(gb[:, 1, :], b.rearrange("(a n) -> a n", a=1).to_broadcast([P, D])).then_inc(gb_loaded, 16)

            for j in range(4):
                load(U_V, 0, j, even_w_in[0, 2 * j * P:2 * (j + 1) * P, 2 * ATT:3 * ATT].rearrange(
                    "(k p) n -> p k n", p=P))
            with sp.Fori(0, 2 * AC // RING) as i:
                for j in range(RING):
                    load(U_Q, i, j, cols(even_w_in[0], RING * i + j))
            load_ln(0, mix_ln_g[0], mix_ln_b[0])
            for i in range(2):
                for j in range(RING):
                    load(U_OUT0, i, j, rows_of(even_w_out[0], (4, 5, 6, 7, 0, 1, 2, 3)[RING * i + j]), False)

            def ffn(l, u_up, u_down, n):
                with sp.Fori(0, FC // 2) as i:
                    for j in range(RING):
                        load(u_up, i, j, cols(ffn_w_up[l], 2 * i + j // 2 + FC * (j % 2)))
                load_ln(n, ffn_ln_g[l], ffn_ln_b[l])
                with sp.Fori(0, FC // RING) as i:
                    for j in range(RING):
                        load(u_down, i, j, rows_of(ffn_w_down[l], RING * i + j), False)
                for j in range(FC % RING):
                    load(u_down, FC // RING, j, rows_of(ffn_w_down[l], FC - FC % RING + j), False)

            ffn(0, U_UP0, U_DOWN0, 1)
            with sp.Fori(0, DC // 2) as i:
                for j in range(RING):
                    load(U_CH, i, j, cols(odd_w_in[0], DC * (1 + j % 2) + 2 * i + j // 2))
            with sp.Fori(0, DC // RING) as i:
                for j in range(RING):
                    load(U_B, i, j, cols(odd_w_in[0], RING * i + j))
            load_ln(2, mix_ln_g[1], mix_ln_b[1])
            with sp.Fori(0, DC // RING) as i:
                for j in range(RING):
                    load(U_OUT1, i, j, rows_of(odd_w_out[0], RING * i + j), False)
            ffn(1, U_UP1, U_DOWN1, 3)
            for s in range(ST):
                sp.wait_ge(x_ready, 3 * ST + s + 1)
                sp.dma_start(out[0, s * P:(s + 1) * P, :], x[:, s, :]).then_inc(out_stored, 16)
            sp.wait_ge(out_stored, 16 * ST)

        @block.gpsimd
        def _(pool):
            pool.memset(ident[:, :], 0.0).then_inc(const_set, 1)
            pool.memset(ident_b[:, :], 0.0).then_inc(const_set, 1)
            pool.memset(mask_b[:, :], 0.0).then_inc(const_set, 1)
            pool.wait_ge(const_set, 3)
            for m in (ident, ident_b):
                pool.affine_select(out=m[:, :], in_=m[:, :], compare_op=ALU.not_equal, fill=1.0, base=0,
                                   pattern=[[-1, P]], channel_multiplier=1).then_inc(const_ready, 1)
            pool.affine_select(out=mask_b[:, :], in_=mask_b[:, :], compare_op=ALU.is_ge, fill=NEG, base=0,
                               pattern=[[-1, P]], channel_multiplier=1).then_inc(const_ready, 1)
            pool.memset(pool_buf[:, :, :], 0.0).then_inc(const_ready, 1)
            for m in (q_hi, q_lo):
                pool.memset(m[:, :, :].bitcast(F32), 0.0).then_inc(const_ready, 1)
            pool.memset(neg_half[:, :], -0.5).then_inc(const_ready, 1)
            pool.iota(inv_count[:, :], pattern=[[1, 16]], base=1, channel_multiplier=0,
                      allow_small_or_imprecise_dtypes=True).then_inc(const_ready, 1)

            def low(u0, i, j):
                u = u0 + RING * i + j
                pool.wait_ge(hi_ready, u + 1)
                sl = slot(u0 + j)
                pool.tensor_tensor(w_lo[:, sl, :], w_raw[:, sl, :], w_hi[:, sl, :].bitcast(F32),
                                   ALU.subtract).then_inc(split_ready, 1)

            def lows(u0, n):
                if n >= 2 * RING:
                    with pool.Fori(0, n // RING) as i:
                        for j in range(RING):
                            low(u0, i, j)
                    u0, n = u0 + n // RING * RING, n % RING
                for j in range(n):
                    low(u0, 0, j)

            def inv_std(n, s):
                k = ST * n + s + 1
                pool.wait_ge(sq_ready, k)
                pool.tensor_scalar(var[:, s:s + 1], vsum[:, s:s + 1], 1.0 / D, EPS,
                                   ALU.mult, ALU.add).then_inc(var_ready, 1)
                pool.wait_ge(var_ready, k)
                pool.tensor_tensor(rstd[:, s:s + 1], var[:, s:s + 1], neg_half[:, :],
                                   ALU.pow).then_inc(rstd_ready, 1)

            def norm_tail(n, u_next):
                for s in range(ST - 1):
                    inv_std(n, s)
                if u_next < UNITS:
                    low(u_next, 0, 0)
                    low(u_next, 0, 1)
                inv_std(n, ST - 1)
                if u_next < UNITS:
                    low(u_next, 0, 2)
                    low(u_next, 0, 3)

            lows(0, U_UP0)
            norm_tail(0, U_UP0)
            lows(U_UP0 + RING, U_CH - U_UP0 - RING)
            norm_tail(1, U_CH)
            lows(U_CH + RING, U_UP1 - U_CH - RING)
            norm_tail(2, U_UP1)
            lows(U_UP1 + RING, UNITS - U_UP1 - RING)
            norm_tail(3, UNITS)

        def h_at(k):
            return h[:, k, :] if isinstance(k, int) else h[:, bass.ds(k, 1), :].rearrange("p a n -> p (a n)")

        def high(act, u0, i, j):
            u = u0 + RING * i + j
            sl = slot(u0 + j)
            act.wait_ge(raw_loaded[sl], 16 * ((u0 + j) // RING + i) + 16)
            if not (isinstance(u, int) and u < RING):
                act.wait_ge(unit_done, u - RING + 1)
            act.activation(w_hi[:, sl, :], w_raw[:, sl, :], ACT.Copy).then_inc(hi_ready, 1)

        TILES = [(e, c) for e in range(2) for c in range(ST)]

        def p_off(c):
            return P * (c * (c + 1) // 2)

        @block.scalar
        def _(act):
            def xt_high(k, s):
                act.wait_ge(xt_ps, k + 1)
                act.activation(xt_hi[:, :, s * P:(s + 1) * P],
                               ps[:, 2 * s:2 * s + 2, :].rearrange("p a (b n) -> p (a b) n", n=P),
                               ACT.Copy).then_inc(xt_hi_ready, 1)

            def norm_square(n, s):
                k = ST * n + s + 1
                act.wait_ge(mu_ready, k)
                act.activation(conv[:, 0, :, :].rearrange("p a n -> p (a n)"), x[:, s, :], ACT.Square,
                               bias=nmu[:, s:s + 1], accum_out=vsum[:, s:s + 1]).then_inc(sq_ready, 1)

            def norm_tail(n, u_next):
                for s in range(ST):
                    if s == ST - 1 and u_next < UNITS:
                        high(act, u_next, 0, 0)
                        high(act, u_next, 0, 1)
                        high(act, u_next, 0, 2)
                    norm_square(n, s)
                    if s and n < 3:
                        xt_high(ST * (n + 1) + s - 1, s - 1)
                if n < 3:
                    high(act, u_next, 0, 3)
                    xt_high(ST * (n + 1) + ST - 1, ST - 1)

            def down(h0, order, u0, nch, n, u_next):
                def post(i, j):
                    high(act, u0 + RING, i, j)
                    jj = RING * i + j + RING
                    act.wait_ge(h_ready, h0 + jj + 1)
                    act.wait_ge(unit_done, u0 + jj - RING + 1)
                    k = order(jj)
                    act.activation(ht_hi[:, j, :], h_at(k), ACT.Copy).then_inc(ht_hi_ready, 1)
                m = nch - TAIL
                if m >= 2 * RING:
                    with act.Fori(0, m // RING) as i:
                        for j in range(RING):
                            post(i, j)
                    for j in range(m % RING):
                        post(m // RING, j)
                else:
                    for j in range(m):
                        post(0, j)
                norm_tail(n, u_next)

            def ht_first(h0, order):
                for j in range(RING):
                    act.wait_ge(h_ready, h0 + j + 1)
                    act.activation(ht_hi[:, j, :], h_at(order(j)), ACT.Copy).then_inc(ht_hi_ready, 1)

            def glu(l, u0, free0, h0):
                wc, bc = col_ffn(l, 2), col_ffn(l, 3)

                def pair(i, q):
                    c = 2 * i + q
                    for e in range(2):
                        high(act, u0 + RING, i, 2 * q + e)
                    act.wait_ge(h_ready, h0 + c - 1)
                    for e in range(2):
                        act.wait_ge(unit_done, u0 + 2 * c + e + 1)
                        act.activation(conv[:, q, e, :], ps[:, 2 * q + e, :], ACT.Identity,
                                       scale=par(c + (wc + e * FC)), bias=par(c + (bc + e * FC))
                                       ).then_inc(conv_base, 1)
                    act.wait_ge(bank_free, free0 + 2 * c + 1)
                    act.activation(act_g[:, q, :], conv[:, q, 0, :], ACT.Silu).then_inc(gate_ready, 1)

                with act.Fori(0, FC // 2 - 1) as i:
                    pair(i, 0)
                    pair(i, 1)
                ht_first(h0, lambda j: j)
                pair(FC // 2 - 1, 0)
                pair(FC // 2 - 1, 1)

            xt_high(0, 0)
            xt_high(1, 1)
            high(act, 0, 0, 0)
            high(act, 0, 0, 1)
            xt_high(2, 2)
            high(act, 0, 0, 2)
            xt_high(3, 3)
            high(act, 0, 0, 3)
            for j in range(RING):
                high(act, U_V, 0, j)
            for j in range(RING):
                high(act, U_Q, 0, j)
            for s in (2, 3):
                act.wait_ge(unit_done, U_Q)
                act.activation(h[:, SLOT_V + s, :], ps[:, 4 + s, :], ACT.Copy).then_inc(v_ready, 1)
            for j in range(RING):
                high(act, U_K, 0, j)
            for j in range(AC):
                high(act, U_OUT0, 0, j)
                act.wait_ge(unit_done, U_K + j + 1)
                act.activation(k_hi[:, j, :], ps[:, j, :], ACT.Copy).then_inc(k_high, 1)

            def exps(p, t):
                e, c = TILES[t % 8]
                act.wait_ge(max_ready, 8 * p + t + 1)
                act.activation(probs[:, e, p_off(c):p_off(c + 1)], ps[:, c, 0:P * (c + 1)], ACT.Exp,
                               bias=neg_max[:, e, c:c + 1],
                               accum_out=prob_sum[:, e, c:c + 1]).then_inc(probs_ready, 1)

            def move(p, t):
                e, c = TILES[t]
                if c in (0, 3):
                    act.wait_ge(pt_done, 8 * p + t + 1)
                    act.activation(probs_t[:, p_off(c):p_off(c + 1)], ps[:, 4 + c % 2, 0:P * (c + 1)],
                                   ACT.Copy).then_inc(pt_act, 1)

            exps(0, 0)
            with act.Fori(0, AC - 1) as p:
                for t in range(1, 9):
                    exps(p, t)
                    move(p, t - 1)
            for t in range(1, 8):
                exps(AC - 1, t)
                move(AC - 1, t - 1)
            move(AC - 1, 7)
            ht_first(H_OUT0, lambda j: j + 4)

            down(H_OUT0, lambda j: (j + 4) % 8, U_OUT0, DC, 0, U_UP0)
            glu(0, U_UP0, FREE_UP0, H_DOWN0)
            down(H_DOWN0, lambda j: j, U_DOWN0, FC, 1, U_CH)

            with act.Fori(0, DC // 2) as i:
                for q in range(2):
                    c = 2 * i + q
                    for e in range(2):
                        high(act, U_CH + RING, i, 2 * q + e)
                    act.wait_ge(unit_done, U_CH + 2 * c + 1)
                    act.wait_ge(bank_free, FREE_CH + 2 * c - 2)
                    act.activation(conv[:, q, 0, :], ps[:, 2 * q, :], ACT.Copy).then_inc(c_ready, 1)
                    act.wait_ge(bank_free, FREE_CH + 2 * c + 2)
                    act.activation(h_at(c), conv[:, q, 1, :], ACT.Identity, scale=par(c + (COL_ODDW + 2 * DC)),
                                   bias=par(c + COL_ODDB)).then_inc(conv_base, 1)
            for j in range(RING):
                high(act, U_B + RING, 0, j)
            ht_first(H_OUT1, lambda j: j)
            for j in range(RING):
                high(act, U_OUT1, 0, j)
            down(H_OUT1, lambda j: j, U_OUT1, DC, 2, U_UP1)
            glu(1, U_UP1, FREE_UP1, H_DOWN1)
            down(H_DOWN1, lambda j: j, U_DOWN1, FC, 3, UNITS)

        @block.vector
        def _(dve):
            def h_part(k, a, b):
                return h[:, bass.ds(k, 1), a:b].rearrange("p a n -> p (a n)")

            def xt_low(k, s):
                dve.wait_ge(xt_hi_ready, k + 1)
                sl = slice(s * P, (s + 1) * P)
                dve.tensor_tensor(xt_lo[:, :, sl],
                                  ps[:, 2 * s:2 * s + 2, :].rearrange("p a (b n) -> p (a b) n", n=P),
                                  xt_hi[:, :, sl].bitcast(F32), ALU.subtract).then_inc(xt_ready, 1)

            def ht_low(h0, order, j, sl):
                dve.wait_ge(ht_hi_ready, h0 + j + 1)
                dve.tensor_tensor(ht_lo[:, sl, :], h_at(order(j)), ht_hi[:, sl, :].bitcast(F32),
                                  ALU.subtract).then_inc(ht_ready, 1)

            def ht_first(h0, order):
                for j in range(RING):
                    ht_low(h0, order, j, j)

            def norm_start(n, s, u_end):
                k = ST * n + s + 1
                if s < ST - 1:
                    dve.wait_ge(tile_done, (ST - 1) * n + s + 1)
                else:
                    dve.wait_ge(unit_done, u_end)
                xs = x[:, s, :].rearrange("p (a n) -> p a n", a=2)
                dve.scalar_tensor_tensor(xs, xs, ALPHA, ps[:, 2 * s:2 * s + 2, :], ALU.mult, ALU.add,
                                         accum_out=zsum[:, s:s + 1]).then_inc(z_ready, 1)
                dve.wait_ge(z_ready, k)
                dve.tensor_scalar(nmu[:, s:s + 1], zsum[:, s:s + 1], -1.0 / D, None,
                                  ALU.mult).then_inc(mu_ready, 1)

            def norm_gain(n, s):
                k = ST * n + s + 1
                dve.wait_ge(mu_ready, k)
                dve.scalar_tensor_tensor(xg, x[:, s, :], nmu[:, s:s + 1], gb[:, 0, :],
                                         ALU.add, ALU.mult).then_inc(xg_ready, 1)

            def norm_end(n, s):
                k = ST * n + s + 1
                dve.wait_ge(xg_ready, k)
                dve.wait_ge(rstd_ready, k)
                dve.scalar_tensor_tensor(x[:, s, :], xg, rstd[:, s:s + 1], gb[:, 1, :],
                                         ALU.mult, ALU.add).then_inc(x_ready, 1)

            def down(h0, order, u0, nch, n):
                m = nch - TAIL
                if m >= 2 * RING:
                    with dve.Fori(0, m // RING) as i:
                        for j in range(RING):
                            ht_low(h0, order, RING * i + (j + RING), j)
                    for j in range(m % RING):
                        ht_low(h0, order, m // RING * RING + j + RING, j)
                else:
                    for j in range(m):
                        ht_low(h0, order, j + RING, j)
                dve.wait_ge(gb_loaded, 32 * (n + 1))
                for s in range(ST):
                    norm_start(n, s, u0 + nch)
                    norm_gain(n, s)
                    norm_end(n, s)
                    if s and n < 3:
                        xt_low(ST * (n + 1) + s - 1, s - 1)
                if n < 3:
                    xt_low(ST * (n + 1) + ST - 1, ST - 1)

            def glu(l, conv0, free0, h0):
                def pair(i, q):
                    c = 2 * i + q
                    for e in range(2):
                        dve.wait_ge(conv_base, conv0 + 2 * c + e + 1)
                        dve.scalar_tensor_tensor(conv[:, q, e, 1:SEQ], ps[:, 2 * q + e, 0:SEQ - 1],
                                                 par(c + (col_ffn(l, 1) + e * FC)), conv[:, q, e, 1:SEQ],
                                                 ALU.mult, ALU.add).then_inc(tap1, 1)
                    for e in range(2):
                        dve.wait_ge(tap1, conv0 + 2 * c + e + 1)
                        dve.scalar_tensor_tensor(conv[:, q, e, 2:SEQ], ps[:, 2 * q + e, 0:SEQ - 2],
                                                 par(c + (col_ffn(l, 0) + e * FC)), conv[:, q, e, 2:SEQ],
                                                 ALU.mult, ALU.add).then_inc(bank_free, 1)
                    dve.wait_ge(bank_free, free0 + 2 * c + 2)
                    dve.wait_ge(gate_ready, FC * l + c + 1)
                    dve.tensor_tensor(h_at(c), act_g[:, q, :], conv[:, q, 1, :],
                                      ALU.mult).then_inc(h_ready, 1)

                with dve.Fori(0, FC // 2 - 1) as i:
                    pair(i, 0)
                    pair(i, 1)
                ht_first(h0, lambda j: j)
                pair(FC // 2 - 1, 0)
                pair(FC // 2 - 1, 1)

            for s in range(ST):
                xt_low(s, s)
            dve.wait_ge(const_ready, 8)
            dve.reciprocal(inv_count[:, :], inv_count[:, :]).then_inc(inv_ready, 1)
            dve.wait_ge(table_t, 1)
            dve.tensor_copy(table[:, :], ps[:, 4, 0:COLS]).then_inc(table_ready, 1)
            dve.wait_ge(inv_ready, 1)

            steps = 0
            for g in range(GROUPS):
                win = 2 << g
                here = slice(PAD, PAD + SEQ)
                u_buf = pool_buf[:, 0, here]
                dve.wait_ge(unit_done, U_POOLIN + g + 1)
                dve.tensor_copy(u_buf, ps[:, g, :]).then_inc(bank_free, 1)
                dve.wait_ge(bank_free, g + 1)
                src = 0
                for i in range(g + 1):
                    dst = 1 + i % 2
                    dve.tensor_tensor(pool_buf[:, dst, here], pool_buf[:, src, here],
                                      pool_buf[:, src, PAD - (1 << i):PAD + SEQ - (1 << i)],
                                      ALU.add).then_inc(pool_step, 1)
                    steps += 1
                    dve.wait_ge(pool_step, steps)
                    src = dst
                dve.scalar_tensor_tensor(pooled[:, g, :], pool_buf[:, src, here], 1.0 / win, u_buf,
                                         ALU.mult, ALU.subtract).then_inc(pool_step, 1)
                n = win - 1
                dve.tensor_tensor(pool_buf[:, 3 - src, PAD:PAD + n], pool_buf[:, src, PAD:PAD + n],
                                  inv_count[:, 0:n], ALU.mult).then_inc(pool_step, 1)
                steps += 2
                dve.wait_ge(pool_step, steps)
                dve.tensor_tensor(pooled[:, g, 0:n], pool_buf[:, 3 - src, PAD:PAD + n],
                                  pool_buf[:, 0, PAD:PAD + n], ALU.subtract).then_inc(pooled_ready, 1)
                dve.wait_ge(pooled_ready, g + 1)

            for s in (0, 1):
                dve.wait_ge(unit_done, U_Q)
                dve.tensor_copy(h[:, SLOT_V + s, :], ps[:, 4 + s, :]).then_inc(v_dve, 1)
            for j in range(AC):
                dve.wait_ge(unit_done, U_Q + j + 1)
                dve.tensor_scalar(h[:, SLOT_Q + j, :], ps[:, j, :], SCALE, None, ALU.mult).then_inc(bank_free, 1)

            def stage_q(p, e):
                half = slice(HEAD_DIM * e, HEAD_DIM * (e + 1))
                src = h[half, bass.ds(p + SLOT_Q, 1), :].rearrange("p a n -> p (a n)")
                dve.tensor_copy(q_hi[half, e, :], src).then_inc(q_high, 1)
                dve.wait_ge(q_high, 2 * p + e + 1)
                dve.tensor_tensor(q_lo[half, e, :], src, q_hi[half, e, :].bitcast(F32),
                                  ALU.subtract).then_inc(q_staged, 1)

            dve.wait_ge(bank_free, 8)
            stage_q(0, 0)
            stage_q(0, 1)
            for j in range(AC):
                dve.wait_ge(k_high, j + 1)
                dve.tensor_tensor(k_lo[:, j, :], ps[:, j, :], k_hi[:, j, :].bitcast(F32),
                                  ALU.subtract).then_inc(bank_free, 1)
            dve.wait_ge(table_ready, 1)
            for g in range(GROUPS):
                dve.wait_ge(mixed_done, g + 1)
                dve.tensor_scalar(h[:, 4 + g, :], ps[:, 4 + g, :], table[:, COL_BPOOL + g:COL_BPOOL + g + 1],
                                  table[:, COL_PSCALE + g:COL_PSCALE + g + 1],
                                  ALU.add, ALU.mult).then_inc(h_ready, 1)

            def top(p, t):
                e, c = TILES[t % 8]
                dve.wait_ge(scores_done, 8 * p + t + 1)
                dve.reduce_max(neg_max[:, e, c:c + 1], ps[:, c, 0:P * (c + 1)], AX_X,
                               negate=True).then_inc(max_ready, 1)

            def move(p, t):
                e, c = TILES[t % 8]
                if c in (1, 2):
                    dve.wait_ge(pt_done, 8 * p + t + 1)
                    dve.tensor_copy(probs_t[:, p_off(c):p_off(c + 1)],
                                    ps[:, 4 + c % 2, 0:P * (c + 1)]).then_inc(pt_dve, 1)

            def head_out(p, e):
                dve.wait_ge(probs_ready, 8 * p + 4 * e + 4)
                dve.reciprocal(prob_inv[:, e, :], prob_sum[:, e, :]).then_inc(inv_sum, 1)
                dve.wait_ge(inv_sum, 2 * p + e + 1)
                dve.wait_ge(o_done, 2 * p + e + 1)
                dst = h[:, SLOT_O:SLOT_O + ST, bass.ds(P * p + HEAD_DIM * e, HEAD_DIM)]
                dve.tensor_tensor(dst, ps[:, 6 + e, 0:ST * HEAD_DIM].rearrange("p (c n) -> p c n", c=ST),
                                  prob_inv[:, e, :].unsqueeze(2).to_broadcast([P, ST, HEAD_DIM]),
                                  ALU.mult).then_inc(o_ready, 1)

            top(0, 0)
            for t in (1, 2):
                top(0, t)
                move(0, t - 1)
            with dve.Fori(0, AC - 1) as p:
                for t in range(3, 11):
                    top(p, t)
                    move(p, t - 1)
                    if t == 4:
                        stage_q(p + 1, 0)
                    if t == 6:
                        head_out(p, 0)
                    if t == 8:
                        stage_q(p + 1, 1)
                    if t == 10:
                        head_out(p, 1)
            for t in range(3, 8):
                top(AC - 1, t)
                move(AC - 1, t - 1)
            head_out(AC - 1, 0)
            head_out(AC - 1, 1)
            ht_first(H_OUT0, lambda j: j + 4)
            for j in range(AC):
                dve.wait_ge(ot_done, j + 1)
                dve.tensor_copy(h[:, j, :], ps[:, j, :]).then_inc(h_ready, 1)

            down(H_OUT0, lambda j: (j + 4) % 8, U_OUT0, DC, 0)
            glu(0, CONV_UP0, FREE_UP0, H_DOWN0)
            down(H_DOWN0, lambda j: j, U_DOWN0, FC, 1)

            with dve.Fori(0, DC // 2) as i:
                for q in range(2):
                    c = 2 * i + q
                    dve.wait_ge(c_ready, c + 1)
                    dve.wait_ge(unit_done, U_CH + 2 * c + 2)
                    dve.tensor_tensor(conv[:, q, 1, :], ps[:, 2 * q + 1, :], conv[:, q, 0, :],
                                      ALU.mult).then_inc(bank_free, 2)
                    dve.wait_ge(conv_base, CONV_CH + c + 1)
                    dve.scalar_tensor_tensor(h_part(c, 1, SEQ), conv[:, q, 1, 0:SEQ - 1],
                                             par(c + (COL_ODDW + DC)), h_part(c, 1, SEQ),
                                             ALU.mult, ALU.add).then_inc(tap1, 1)
                    dve.wait_ge(tap1, CONV_CH + c + 1)
                    dve.scalar_tensor_tensor(h_part(c, 2, SEQ), conv[:, q, 1, 0:SEQ - 2],
                                             par(c + COL_ODDW), h_part(c, 2, SEQ),
                                             ALU.mult, ALU.add).then_inc(short_ready, 1)
            dve.wait_ge(short_ready, DC)
            for j in range(DC):
                if j == RING:
                    ht_first(H_OUT1, lambda j: j)
                dve.wait_ge(unit_done, U_B + j + 1)
                dve.tensor_tensor(h[:, j, :], ps[:, j % RING, :], h[:, j, :], ALU.mult).then_inc(h_ready, 1)
            down(H_OUT1, lambda j: j, U_OUT1, DC, 2)
            glu(1, CONV_UP1, FREE_UP1, H_DOWN1)
            down(H_DOWN1, lambda j: j, U_DOWN1, FC, 3)

        @block.tensor
        def _(pe):
            def three(dst, a_hi, a_lo, b_hi, b_lo, start, stop):
                pe.matmul(dst, a_hi, b_hi, start=start, stop=False)
                pe.matmul(dst, a_hi, b_lo, start=False, stop=False)
                return pe.matmul(dst, a_lo, b_hi, start=False, stop=stop)

            def x_transpose(s):
                for d in range(DC):
                    last = pe.transpose(ps[:, 2 * s + d // 4, (d % 4) * P:(d % 4 + 1) * P],
                                        x[:, s, d * P:(d + 1) * P], ident[:, :])
                last.then_inc(xt_ps, 1)

            def up_part(u0, j, bank, a, b):
                sl = slot(u0 + j)
                for k in range(DC):
                    ks = slice(k * P, (k + 1) * P)
                    last = three(ps[:, bank, a:b], w_hi[:, sl, ks], w_lo[:, sl, ks],
                                 xt_hi[:, k, a:b], xt_lo[:, k, a:b], k == 0, k == DC - 1)
                return last

            def up_unit(u0, i, j, bank):
                pe.wait_ge(split_ready, u0 + RING * i + (j + 1))
                up_part(u0, j, bank, 0, SEQ).then_inc(unit_done, 1)

            def up_first(u0, xt0, tile_wait):
                pe.wait_ge(xt_ready, xt0 + 2)
                for j in range(RING):
                    pe.wait_ge(split_ready, u0 + j + 1)
                    up_part(u0, j, j, 0, SEQ // 2)
                    if j in (0, 2):
                        pe.wait_ge(*tile_wait(2 + j // 2))
                        x_transpose(2 + j // 2)
                pe.wait_ge(xt_ready, xt0 + ST)
                for j in range(RING):
                    up_part(u0, j, j, SEQ // 2, SEQ).then_inc(unit_done, 1)

            def down_part(sl, j, s, start, stop):
                ss = slice(s * P, (s + 1) * P)
                for n in range(2):
                    ns = slice(n * 512, (n + 1) * 512)
                    last = three(ps[:, 2 * s + n, :], ht_hi[:, j, ss], ht_lo[:, j, ss],
                                 w_hi[:, sl, ns], w_lo[:, sl, ns], start, stop)
                return last

            def down(h0, u0, nch, n, banks_read):
                def unit(i, j, first=False):
                    u = u0 + RING * i + j
                    pe.wait_ge(split_ready, u + 1)
                    pe.wait_ge(ht_ready, h0 + RING * i + (j + 1))
                    for s in (2, 3, 0, 1):
                        if first and s == 0:
                            pe.wait_ge(*banks_read)
                        last = down_part(slot(u0 + j), j, s, first, False)
                    last.then_inc(unit_done, 1)

                m = nch - TAIL
                for j in range(RING):
                    unit(0, j, j == 0)
                if m >= 2 * RING:
                    with pe.Fori(1, m // RING) as i:
                        for j in range(RING):
                            unit(i, j)
                    for j in range(m % RING):
                        unit(m // RING, j)
                for s in range(ST):
                    for j in range(m, nch):
                        if s == 0:
                            pe.wait_ge(split_ready, u0 + j + 1)
                            pe.wait_ge(ht_ready, h0 + j + 1)
                        last = down_part(slot(u0 + j), j % RING, s, False, j == nch - 1)
                        if s == ST - 1:
                            last.then_inc(unit_done, 1)
                        if s >= 2 and j == m and n < 3:
                            pe.wait_ge(x_ready, ST * n + s - 1)
                            x_transpose(s - 2)
                    if s < ST - 1:
                        last.then_inc(tile_done, 1)

            def next_up(u0, n):
                up_first(u0, ST * (n + 1), lambda s: (x_ready, ST * n + s + 1))

            def glu(u0, free0, n):
                next_up(u0, n)
                with pe.Fori(1, FC // 2) as i:
                    for j in range(RING):
                        pe.wait_ge(bank_free, RING * i + (free0 + j + 1 - RING))
                        up_unit(u0, i, j, j)

            pe.wait_ge(const_ready, 1)
            for s in (0, 1):
                pe.wait_ge(x_loaded[s], 16)
                x_transpose(s)
            up_first(U_POOLIN, 0, lambda s: (x_loaded[s], 16))
            pe.wait_ge(rows_loaded, 16 * (3 * DEPTH + 4))
            for r in range(5):
                n, at = (2 * NF, 2 * NF * r) if r < 4 else (COLS - COL_BPOOL, COL_BPOOL)
                last = pe.transpose(ps[:, 4, at:at + n], rows[0:n, r, :], ident[0:n, 0:n])
            last.then_inc(table_t, 1)

            for j in range(4):
                pe.wait_ge(split_ready, U_V + j + 1)
                for s in (1, 2, 3, 0):
                    ss = slice(s * P, (s + 1) * P)
                    if j == 0 and s == 0:
                        pe.wait_ge(table_ready, 1)
                    for kk in range(2):
                        ns = slice(kk * ATT, (kk + 1) * ATT)
                        k = 2 * j + kk
                        last = three(ps[:, 4 + s, :], xt_hi[:, k, ss], xt_lo[:, k, ss],
                                     w_hi[:, j, ns], w_lo[:, j, ns], k == 0, k == DC - 1)
                last.then_inc(unit_done, 1)
            with pe.Fori(0, 2) as i:
                for j in range(RING):
                    pe.wait_ge(bank_free, RING * i + j + 1)
                    up_unit(U_Q, i, j, j)
            pe.wait_ge(wpool_loaded, 16)
            pe.wait_ge(v_dve, 2)
            pe.wait_ge(v_ready, 2)
            for g in range(GROUPS):
                pe.wait_ge(pooled_ready, g + 1)
                pe.matmul(ps[:, 4 + g, :], wpool[:, g, :], pooled[:, g, :], start=True, stop=True
                          ).then_inc(mixed_done, 1)

            def scores(p, t):
                e, c = TILES[t % 8]
                width = P * (c + 1)
                qs = slice(c * P, (c + 1) * P)
                pair = bass.ds(p + t // 8, 1)
                three(ps[:, c, 0:width], q_hi[:, e, qs], q_lo[:, e, qs],
                      k_hi[:, pair, 0:width].rearrange("p a n -> p (a n)"),
                      k_lo[:, pair, 0:width].rearrange("p a n -> p (a n)"), True, False)
                pe.matmul(ps[:, c, c * P:width], ident_b[:, :], mask_b[:, :],
                          start=False, stop=True).then_inc(scores_done, 1)

            def transposed(p, t):
                e, c = TILES[t % 8]
                pe.wait_ge(probs_ready, 8 * p + t + 1)
                for kc in range(c + 1):
                    last = pe.transpose(ps[:, 4 + c % 2, kc * P:(kc + 1) * P],
                                        probs[:, e, p_off(c) + kc * P:p_off(c) + (kc + 1) * P], ident[:, :])
                last.then_inc(pt_done, 1)

            def outputs(p, t):
                e, c = TILES[t]
                if c in (0, 3):
                    pe.wait_ge(pt_act, 4 * p + 2 * e + (1 if c == 0 else 2))
                else:
                    pe.wait_ge(pt_dve, 4 * p + 2 * e + c)
                for kc in range(c + 1):
                    at = p_off(c) + kc * P
                    last = pe.matmul(ps[:, 6 + e, c * HEAD_DIM:(c + 1) * HEAD_DIM], probs_t[:, at:at + P],
                                     h[:, SLOT_V + kc, bass.ds(P * p + HEAD_DIM * e, HEAD_DIM)],
                                     start=(kc == 0), stop=(kc == c))
                if c == ST - 1:
                    last.then_inc(o_done, 1)

            def step(p, t, more):
                if t + 3 < 8 or more:
                    if (t + 3) % 4 == 0:
                        pe.wait_ge(q_staged, 2 * p + (t + 3) // 4 + 1)
                    scores(p, t + 3)
                transposed(p, t)
                outputs(p, t - 1)

            pe.wait_ge(q_staged, 1)
            pe.wait_ge(bank_free, 12)
            for t in range(4):
                scores(0, t)
            pe.wait_ge(h_ready, 4)
            transposed(0, 0)
            with pe.Fori(0, AC - 1) as p:
                for t in range(1, 9):
                    step(p, t, True)
            for t in range(1, 8):
                step(AC - 1, t, False)
            outputs(AC - 1, 7)
            pe.wait_ge(o_ready, 2 * AC)
            for j in range(AC):
                for s in range(ST):
                    last = pe.transpose(ps[:, j, s * P:(s + 1) * P], o_nat[:, s, j * P:(j + 1) * P], ident[:, :])
                last.then_inc(ot_done, 1)

            down(H_OUT0, U_OUT0, DC, 0, (h_ready, H_DOWN0))
            glu(U_UP0, FREE_UP0, 0)
            down(H_DOWN0, U_DOWN0, FC, 1, (bank_free, FREE_CH))
            next_up(U_CH, 1)
            with pe.Fori(1, DC // 2) as i:
                for j in range(RING):
                    pe.wait_ge(bank_free, RING * i + (FREE_CH + 2 * (j // 2) - 2))
                    up_unit(U_CH, i, j, j)
            for j in range(DC):
                if j < RING:
                    pe.wait_ge(bank_free, FREE_UP1)
                else:
                    pe.wait_ge(h_ready, H_OUT1 + j - RING + 1)
                up_unit(U_B, 0, j, j % RING)
            down(H_OUT1, U_OUT1, DC, 2, (h_ready, H_DOWN1))
            glu(U_UP1, FREE_UP1, 2)
            down(H_DOWN1, U_DOWN1, FC, 3, (bank_free, FREE_END))


_INS = ["x", "even_w_in", "even_w_pool", "even_b_pool", "even_pool_scale", "even_w_out",
        "odd_w_in", "odd_conv_w", "odd_conv_b", "odd_w_out", "mix_ln_g", "mix_ln_b",
        "ffn_w_up", "ffn_conv_w", "ffn_conv_b", "ffn_w_down", "ffn_ln_g", "ffn_ln_b"]


def kernel(**inputs):
    import numpy as _np
    import concourse.bacc as _bacc
    from concourse import mybir as _mybir
    from concourse.bass_utils import run_bass_kernel_spmd as _run

    nc = _bacc.Bacc("TRN2", target_bir_lowering=False, num_devices=1)
    arrays, args = {}, []
    for name in _INS:
        a = _np.ascontiguousarray(inputs[name])
        arrays[f"in_{name}"] = a
        args.append(nc.dram_tensor(f"in_{name}", a.shape, _mybir.dt.from_np(a.dtype), kind="ExternalInput").ap())
    out = nc.dram_tensor("out_x", inputs["x"].shape, _mybir.dt.float32, kind="ExternalOutput").ap()
    trunk_program(nc, *args, out)
    return _run(nc, [arrays], core_ids=[0]).results[0]["out_x"]
```

```python
from contextlib import ExitStack

import concourse.bass as bass
from concourse import mybir

ALU = mybir.AluOpType
ACT = mybir.ActivationFunctionType
F32 = mybir.dt.float32
F32R = mybir.dt.float32r
BF16 = mybir.dt.bfloat16
AX_X = mybir.AxisListType.X
P = 128


def trunk_program(nc, FC, x_in, xt_in, units, wpool_in, table_in, ln_in, out):
    SEQ, D = x_in.shape
    LNS = ln_in.shape[0]
    DEPTH = LNS // 2
    UNITS = units.shape[0]
    ATT = D // 2
    HEAD_DIM = 64
    ST = SEQ // P
    DC = D // P
    AC = ATT // P
    GROUPS = AC
    ALPHA = float((2 * DEPTH) ** 0.25)
    EPS = 1e-5
    NEG = -1e30
    SCALE = float(HEAD_DIM) ** -0.5
    RING = 4
    TAIL = 4
    PAD = 8
    BANKS = 8
    assert (SEQ, D, DEPTH, FC % 2) == (512, 1024, 2, 0)

    U_POOLIN, U_V, U_Q, U_K = 0, 4, 8, 12
    U_OUT0 = 16
    U_UP0 = U_OUT0 + DC
    U_DOWN0 = U_UP0 + 2 * FC
    U_CH = U_DOWN0 + FC
    U_B = U_CH + 2 * DC
    U_OUT1 = U_B + DC
    U_UP1 = U_OUT1 + DC
    U_DOWN1 = U_UP1 + 2 * FC
    assert UNITS == U_DOWN1 + FC

    FREE_UP0 = 12
    FREE_CH = FREE_UP0 + 2 * FC
    FREE_UP1 = FREE_CH + 2 * DC
    FREE_END = FREE_UP1 + 2 * FC
    H_OUT0 = 0
    H_DOWN0 = H_OUT0 + DC
    H_OUT1 = H_DOWN0 + FC
    H_DOWN1 = H_OUT1 + DC
    CONV_UP0, CONV_CH, CONV_UP1 = 0, 2 * FC, 2 * FC + DC

    SLOT_O, SLOT_Q, SLOT_V = DC, DC + AC, DC + 2 * AC

    NF = 2 * FC

    def col_ffn(layer, tap):
        return (layer * 4 + tap) * NF
    COL_BPOOL = DEPTH * 4 * NF
    COL_PSCALE = COL_BPOOL + GROUPS
    COL_ODDW = COL_PSCALE + GROUPS
    COL_ODDB = COL_ODDW + 3 * DC
    COLS = COL_ODDB + DC
    assert table_in.shape == (P, COLS)

    with ExitStack() as ctx:
        def sb(name, shape, dt=F32):
            return ctx.enter_context(nc.sbuf_tensor(name, shape, dt))

        def sem(name):
            return ctx.enter_context(nc.semaphore(name))

        ps = ctx.enter_context(nc.psum_tensor("ps", [P, BANKS, 512], F32))

        w_raw = sb("w_raw", [P, RING, D])
        w_hi = sb("w_hi", [P, RING, D], F32R)
        w_lo = sb("w_lo", [P, RING, D], F32R)
        xt_hi = sb("xt_hi", [P, DC, SEQ], F32R)
        xt_lo = sb("xt_lo", [P, DC, SEQ], F32R)
        x = sb("x", [P, ST, D])
        h = sb("h", [P, FC, SEQ])
        ht_hi = sb("ht_hi", [P, RING, SEQ], F32R)
        ht_lo = sb("ht_lo", [P, RING, SEQ], F32R)
        gb = sb("gb", [P, 2, D])
        conv = sb("conv", [P, 2, 2, SEQ])
        act_g = sb("act_g", [P, 2, SEQ])
        probs = sb("probs", [P, 2, 1280])
        probs_t = sb("probs_t", [P, 1280])
        q_hi = sb("q_hi", [P, 2, SEQ], F32R)
        q_lo = sb("q_lo", [P, 2, SEQ], F32R)
        wpool = sb("wpool", [P, GROUPS, P])
        table = sb("table", [P, COLS])
        ident = sb("ident", [P, P])
        ident_b = sb("ident_b", [P, P], BF16)
        mask_b = sb("mask_b", [P, P], BF16)
        inv_count = sb("inv_count", [P, 16])
        stats = sb("stats", [P, 5, ST])
        last_stat = sb("last_stat", [P, 14])
        neg_half = sb("neg_half", [P, 1])
        att_stat = sb("att_stat", [P, 3, 2, ST])

        pool_buf = probs[:, :, :].rearrange("p a b -> p (a b)")[:, 0:3 * (PAD + SEQ)].rearrange(
            "p (a b) -> p a b", a=3)
        xg = act_g[:, :, :].rearrange("p a n -> p (a n)")
        o_nat = h[:, SLOT_O:SLOT_O + ST, :]
        pooled = o_nat
        k_hi, k_lo = ht_hi, ht_lo

        zsum, nmu, vsum, var, rstd = (stats[:, i, :] for i in range(5))
        neg_max, prob_sum, prob_inv = (att_stat[:, i, :, :] for i in range(3))

        raw_loaded = [sem(f"raw_loaded{i}") for i in range(RING)]
        xt_loaded = [sem(f"xt_loaded{i}") for i in range(4)]
        x_loaded = sem("x_loaded")
        table_loaded = sem("table_loaded")
        wpool_loaded = sem("wpool_loaded")
        gb_loaded = sem("gb_loaded")
        out_stored = sem("out_stored")
        const_set = sem("const_set")
        const_ready = sem("const_ready")
        inv_ready = sem("inv_ready")
        hi_ready = sem("hi_ready")
        split_ready = sem("split_ready")
        unit_done = sem("unit_done")
        bank_free = sem("bank_free")
        xt_ps = sem("xt_ps")
        xt_hi_ready = sem("xt_hi_ready")
        xt_ready = sem("xt_ready")
        h_ready = sem("h_ready")
        ht_hi_ready = sem("ht_hi_ready")
        ht_ready = sem("ht_ready")
        pool_step = sem("pool_step")
        pooled_ready = sem("pooled_ready")
        mixed_done = sem("mixed_done")
        v_ready = sem("v_ready")
        v_dve = sem("v_dve")
        q_high = sem("q_high")
        q_staged = sem("q_staged")
        k_high = sem("k_high")
        scores_done = sem("scores_done")
        max_ready = sem("max_ready")
        probs_ready = sem("probs_ready")
        pt_done = sem("pt_done")
        pt_act = sem("pt_act")
        pt_dve = sem("pt_dve")
        o_done = sem("o_done")
        inv_sum = sem("inv_sum")
        o_ready = sem("o_ready")
        ot_done = sem("ot_done")
        conv_base = sem("conv_base")
        tap1 = sem("tap1")
        gate_ready = sem("gate_ready")
        c_ready = sem("c_ready")
        short_ready = sem("short_ready")
        tile_done = sem("tile_done")
        half_done = sem("half_done")
        last_bn = sem("last_bn")
        last_var = sem("last_var")
        z_ready = sem("z_ready")
        mu_ready = sem("mu_ready")
        sq_ready = sem("sq_ready")
        var_ready = sem("var_ready")
        rstd_ready = sem("rstd_ready")
        xg_ready = sem("xg_ready")
        x_ready = sem("x_ready")

        def piece(t, i):
            n, k = i // 2, i % 2
            return t[:, k * DC // 2:(k + 1) * DC // 2, n * SEQ // 2:(n + 1) * SEQ // 2]

        def par(c):
            return table[:, bass.ds(c, 1)]

        def slot(u):
            return u % RING

        block = ctx.enter_context(nc.Block())

        @block.sync
        def _(sp):
            def load(u0, i, j):
                u = u0 + RING * i + j
                if isinstance(u, int):
                    src = units[u, :, :]
                else:
                    src = units[bass.ds(u, 1), :, :].rearrange("a p n -> p (a n)")
                if not (isinstance(u, int) and u < RING):
                    sp.wait_ge(split_ready, u - RING + 1)
                sp.dma_start(w_raw[:, slot(u0 + j), :], src).then_inc(raw_loaded[slot(u0 + j)], 16)

            def loads(u0, end):
                n = end - u0
                with sp.Fori(0, n // RING) as i:
                    for j in range(RING):
                        load(u0, i, j)
                for j in range(n % RING):
                    load(u0 + n // RING * RING, 0, j)

            def load_xt(i):
                sp.dma_start(piece(h, i), xt_in[i // 2, i % 2, :, :, :]).then_inc(xt_loaded[i], 16)

            def load_ln(n):
                if n:
                    sp.wait_ge(x_ready, ST * n)
                for a in range(2):
                    sp.dma_start(gb[:, a, :], ln_in[n, a:a + 1, :].to_broadcast([P, D])).then_inc(gb_loaded, 16)

            load(0, 0, 0)
            load_xt(0)
            load_xt(1)
            load(0, 0, 1)
            load_xt(2)
            load_xt(3)
            load(0, 0, 2)
            load(0, 0, 3)
            sp.dma_start(table[:, :], table_in[:, :]).then_inc(table_loaded, 16)
            sp.dma_start(wpool[:, :, :], wpool_in[:, :, :]).then_inc(wpool_loaded, 16)
            loads(RING, U_OUT0)
            sp.dma_start(x[:, :, :], x_in.rearrange("(s p) d -> p s d", p=P)).then_inc(x_loaded, 16)
            load_ln(0)
            loads(U_OUT0, U_DOWN0)
            load_ln(1)
            loads(U_DOWN0, U_OUT1)
            load_ln(2)
            loads(U_OUT1, U_DOWN1)
            load_ln(3)
            loads(U_DOWN1, UNITS)
            for s in range(ST - 1):
                sp.wait_ge(x_ready, 3 * ST + s + 1)
                sp.dma_start(out[s * P:(s + 1) * P, :], x[:, s, :]).then_inc(out_stored, 16)
            for a in range(2):
                s, cs = ST - 1, slice(512 * a, 512 * (a + 1))
                sp.wait_ge(x_ready, 4 * ST + a)
                sp.dma_start(out[s * P:(s + 1) * P, cs], x[:, s, cs]).then_inc(out_stored, 16)
            sp.wait_ge(out_stored, 16 * (ST + 1))

        @block.gpsimd
        def _(pool):
            def low(u0, i, j):
                u = u0 + RING * i + j
                pool.wait_ge(hi_ready, u + 1)
                sl = slot(u0 + j)
                pool.tensor_tensor(w_lo[:, sl, :], w_raw[:, sl, :], w_hi[:, sl, :].bitcast(F32),
                                   ALU.subtract).then_inc(split_ready, 1)

            def lows(u0, n):
                if n >= 2 * RING:
                    with pool.Fori(0, n // RING) as i:
                        for j in range(RING):
                            low(u0, i, j)
                    u0, n = u0 + n // RING * RING, n % RING
                for j in range(n):
                    low(u0, 0, j)

            pool.memset(ident[:, :], 0.0).then_inc(const_set, 1)
            pool.memset(ident_b[:, :], 0.0).then_inc(const_set, 1)
            pool.memset(mask_b[:, :], 0.0).then_inc(const_set, 1)
            pool.wait_ge(const_set, 3)
            for m in (ident, ident_b):
                pool.affine_select(out=m[:, :], in_=m[:, :], compare_op=ALU.not_equal, fill=1.0, base=0,
                                   pattern=[[-1, P]], channel_multiplier=1).then_inc(const_ready, 1)
            pool.affine_select(out=mask_b[:, :], in_=mask_b[:, :], compare_op=ALU.is_ge, fill=NEG, base=0,
                               pattern=[[-1, P]], channel_multiplier=1).then_inc(const_ready, 1)
            lows(0, RING)
            pool.memset(pool_buf[:, :, :], 0.0).then_inc(const_ready, 1)
            for m in (q_hi, q_lo):
                pool.memset(m[:, :, :].bitcast(F32), 0.0).then_inc(const_ready, 1)
            pool.memset(neg_half[:, :], -0.5).then_inc(const_ready, 1)
            pool.iota(inv_count[:, :], pattern=[[1, 16]], base=1, channel_multiplier=0,
                      allow_small_or_imprecise_dtypes=True).then_inc(const_ready, 1)

            def inv_std(n, s):
                k = ST * n + s + 1
                pool.wait_ge(sq_ready, k)
                pool.tensor_scalar(var[:, s:s + 1], vsum[:, s:s + 1], 1.0 / D, EPS,
                                   ALU.mult, ALU.add).then_inc(var_ready, 1)
                pool.wait_ge(var_ready, k)
                pool.tensor_tensor(rstd[:, s:s + 1], var[:, s:s + 1], neg_half[:, :],
                                   ALU.pow).then_inc(rstd_ready, 1)

            def norm_tail(n, u_next):
                inv_std(n, 0)
                inv_std(n, 1)
                if u_next < UNITS:
                    low(u_next, 0, 0)
                inv_std(n, 2)
                if u_next < UNITS:
                    low(u_next, 0, 1)
                    low(u_next, 0, 2)
                    inv_std(n, 3)
                    low(u_next, 0, 3)

            lows(RING, U_UP0 - RING)
            norm_tail(0, U_UP0)
            lows(U_UP0 + RING, U_CH - U_UP0 - RING)
            norm_tail(1, U_CH)
            lows(U_CH + RING, U_UP1 - U_CH - RING)
            norm_tail(2, U_UP1)
            lows(U_UP1 + RING, UNITS - U_UP1 - RING)
            norm_tail(3, UNITS)
            pool.wait_ge(last_var, 1)
            pool.tensor_scalar(var[:, ST - 1:ST], last_stat[:, 13:14], 1.0, EPS,
                               ALU.mult, ALU.add).then_inc(var_ready, 1)
            pool.wait_ge(var_ready, 4 * ST)
            pool.tensor_tensor(rstd[:, ST - 1:ST], var[:, ST - 1:ST], neg_half[:, :],
                               ALU.pow).then_inc(rstd_ready, 1)

        def h_at(k):
            return h[:, k, :] if isinstance(k, int) else h[:, bass.ds(k, 1), :].rearrange("p a n -> p (a n)")

        def high(act, u0, i, j):
            u = u0 + RING * i + j
            sl = slot(u0 + j)
            act.wait_ge(raw_loaded[sl], 16 * ((u0 + j) // RING + i) + 16)
            if not (isinstance(u, int) and u < RING):
                act.wait_ge(unit_done, u - RING + 1)
            act.activation(w_hi[:, sl, :], w_raw[:, sl, :], ACT.Copy).then_inc(hi_ready, 1)

        TILES = [(e, c) for e in range(2) for c in range(ST)]

        def p_off(c):
            return P * (c * (c + 1) // 2)

        @block.scalar
        def _(act):
            def xt_high(k, s):
                act.wait_ge(xt_ps, k + 1 - ST)
                act.activation(xt_hi[:, :, s * P:(s + 1) * P],
                               ps[:, 2 * s:2 * s + 2, :].rearrange("p a (b n) -> p (a b) n", n=P),
                               ACT.Copy).then_inc(xt_hi_ready, 1)

            def norm_square(n, s):
                k = ST * n + s + 1
                act.wait_ge(mu_ready, k)
                act.activation(conv[:, 0, :, :].rearrange("p a n -> p (a n)"), x[:, s, :], ACT.Square,
                               bias=nmu[:, s:s + 1], accum_out=vsum[:, s:s + 1]).then_inc(sq_ready, 1)

            def norm_tail(n, u_next):
                for s in range(ST):
                    if u_next < UNITS:
                        if s == ST - 2:
                            high(act, u_next, 0, 0)
                        if s == ST - 1:
                            high(act, u_next, 0, 1)
                            high(act, u_next, 0, 2)
                    if n < 3 or s < ST - 1:
                        norm_square(n, s)
                    if s and n < 3:
                        xt_high(ST * (n + 1) + s - 1, s - 1)
                if n < 3:
                    high(act, u_next, 0, 3)
                    xt_high(ST * (n + 1) + ST - 1, ST - 1)

            def down(h0, order, u0, nch, n, u_next):
                def post(i, j):
                    high(act, u0 + RING, i, j)
                    jj = RING * i + j + RING
                    act.wait_ge(h_ready, h0 + jj + 1)
                    act.wait_ge(unit_done, u0 + jj - RING + 1)
                    k = order(jj)
                    act.activation(ht_hi[:, j, :], h_at(k), ACT.Copy).then_inc(ht_hi_ready, 1)
                m = nch - TAIL
                if m >= 2 * RING:
                    with act.Fori(0, m // RING) as i:
                        for j in range(RING):
                            post(i, j)
                    for j in range(m % RING):
                        post(m // RING, j)
                else:
                    for j in range(m):
                        post(0, j)
                norm_tail(n, u_next)

            def ht_first(h0, order, js=range(RING)):
                for j in js:
                    act.wait_ge(h_ready, h0 + j + 1)
                    act.activation(ht_hi[:, j, :], h_at(order(j)), ACT.Copy).then_inc(ht_hi_ready, 1)

            def glu(l, u0, free0, h0):
                wc, bc = col_ffn(l, 2), col_ffn(l, 3)

                def pair(i, q, last=False):
                    c = 2 * i + q
                    if not last:
                        for e in range(2):
                            high(act, u0 + RING, i, 2 * q + e)
                    act.wait_ge(h_ready, h0 + c - 1)
                    for e in range(2):
                        act.wait_ge(unit_done, u0 + 2 * c + e + 1)
                        act.activation(conv[:, q, e, :], ps[:, 2 * q + e, :], ACT.Identity,
                                       scale=par(c + (wc + e * FC)), bias=par(c + (bc + e * FC))
                                       ).then_inc(conv_base, 1)
                    act.wait_ge(bank_free, free0 + 2 * c + 1)
                    act.activation(act_g[:, q, :], conv[:, q, 0, :], ACT.Silu).then_inc(gate_ready, 1)
                    if last:
                        for e in range(2):
                            high(act, u0 + RING, i, 2 * q + e)

                with act.Fori(0, FC // 2 - 1) as i:
                    pair(i, 0)
                    pair(i, 1)
                ht_first(h0, lambda j: j)
                pair(FC // 2 - 1, 0)
                pair(FC // 2 - 1, 1, last=True)

            def xt_first(i):
                act.wait_ge(xt_loaded[i], 16)
                act.activation(piece(xt_hi, i), piece(h, i), ACT.Copy).then_inc(xt_hi_ready, 1)

            high(act, 0, 0, 0)
            xt_first(0)
            xt_first(1)
            high(act, 0, 0, 1)
            xt_first(2)
            xt_first(3)
            high(act, 0, 0, 2)
            high(act, 0, 0, 3)
            for j in range(RING):
                high(act, U_V, 0, j)
            for j in range(RING):
                high(act, U_Q, 0, j)
            for s in (2, 3):
                act.wait_ge(unit_done, U_Q)
                act.activation(h[:, SLOT_V + s, :], ps[:, 4 + s, :], ACT.Copy).then_inc(v_ready, 1)
            for j in range(RING):
                high(act, U_K, 0, j)
            for j in range(AC):
                high(act, U_OUT0, 0, j)
                act.wait_ge(unit_done, U_K + j + 1)
                act.activation(k_hi[:, j, :], ps[:, j, :], ACT.Copy).then_inc(k_high, 1)

            def exps(p, t):
                e, c = TILES[t % 8]
                act.wait_ge(max_ready, 8 * p + t + 1)
                act.activation(probs[:, e, p_off(c):p_off(c + 1)], ps[:, c, 0:P * (c + 1)], ACT.Exp,
                               bias=neg_max[:, e, c:c + 1],
                               accum_out=prob_sum[:, e, c:c + 1]).then_inc(probs_ready, 1)

            def move(p, t):
                e, c = TILES[t]
                if c in (0, 3):
                    act.wait_ge(pt_done, 8 * p + t + 1)
                    act.activation(probs_t[:, p_off(c):p_off(c + 1)], ps[:, 4 + c % 2, 0:P * (c + 1)],
                                   ACT.Copy).then_inc(pt_act, 1)

            exps(0, 0)
            with act.Fori(0, AC - 1) as p:
                for t in range(1, 9):
                    exps(p, t)
                    move(p, t - 1)
            for t in range(1, 8):
                exps(AC - 1, t)
                move(AC - 1, t - 1)
                if t == 3:
                    ht_first(H_OUT0, lambda j: j + 4, (0,))
            move(AC - 1, 7)
            ht_first(H_OUT0, lambda j: j + 4, (1, 2, 3))

            down(H_OUT0, lambda j: (j + 4) % 8, U_OUT0, DC, 0, U_UP0)
            act.wait_ge(table_loaded, 16)
            act.activation(att_stat[:, 0, 0, 0:1], table[:, 0:1], ACT.Silu)
            glu(0, U_UP0, FREE_UP0, H_DOWN0)
            down(H_DOWN0, lambda j: j, U_DOWN0, FC, 1, U_CH)

            with act.Fori(0, DC // 2) as i:
                for q in range(2):
                    c = 2 * i + q
                    for e in range(2):
                        high(act, U_CH + RING, i, 2 * q + e)
                    act.wait_ge(unit_done, U_CH + 2 * c + 1)
                    act.wait_ge(bank_free, FREE_CH + 2 * c - 2)
                    act.activation(conv[:, q, 0, :], ps[:, 2 * q, :], ACT.Copy).then_inc(c_ready, 1)
                    act.wait_ge(bank_free, FREE_CH + 2 * c + 2)
                    act.activation(h_at(c), conv[:, q, 1, :], ACT.Identity, scale=par(c + (COL_ODDW + 2 * DC)),
                                   bias=par(c + COL_ODDB)).then_inc(conv_base, 1)
            for j in range(RING):
                high(act, U_B + RING, 0, j)
            ht_first(H_OUT1, lambda j: j)
            for j in range(RING):
                high(act, U_OUT1, 0, j)
            down(H_OUT1, lambda j: j, U_OUT1, DC, 2, U_UP1)
            glu(1, U_UP1, FREE_UP1, H_DOWN1)
            down(H_DOWN1, lambda j: j, U_DOWN1, FC, 3, UNITS)

        @block.vector
        def _(dve):
            def h_part(k, a, b):
                return h[:, bass.ds(k, 1), a:b].rearrange("p a n -> p (a n)")

            def xt_low(k, s):
                dve.wait_ge(xt_hi_ready, k + 1)
                sl = slice(s * P, (s + 1) * P)
                dve.tensor_tensor(xt_lo[:, :, sl],
                                  ps[:, 2 * s:2 * s + 2, :].rearrange("p a (b n) -> p (a b) n", n=P),
                                  xt_hi[:, :, sl].bitcast(F32), ALU.subtract).then_inc(xt_ready, 1)

            def ht_low(h0, order, j, sl):
                dve.wait_ge(ht_hi_ready, h0 + j + 1)
                dve.tensor_tensor(ht_lo[:, sl, :], h_at(order(j)), ht_hi[:, sl, :].bitcast(F32),
                                  ALU.subtract).then_inc(ht_ready, 1)

            def ht_first(h0, order, js=range(RING)):
                for j in js:
                    ht_low(h0, order, j, j)

            def norm_start(n, s, u_end):
                k = ST * n + s + 1
                if s < ST - 1:
                    dve.wait_ge(tile_done, (ST - 1) * n + s + 1)
                else:
                    dve.wait_ge(unit_done, u_end)
                xs = x[:, s, :].rearrange("p (a n) -> p a n", a=2)
                dve.scalar_tensor_tensor(xs, xs, ALPHA, ps[:, 2 * s:2 * s + 2, :], ALU.mult, ALU.add,
                                         accum_out=zsum[:, s:s + 1]).then_inc(z_ready, 1)
                dve.wait_ge(z_ready, k)
                dve.tensor_scalar(nmu[:, s:s + 1], zsum[:, s:s + 1], -1.0 / D, None,
                                  ALU.mult).then_inc(mu_ready, 1)

            def norm_gain(n, s):
                k = ST * n + s + 1
                dve.wait_ge(mu_ready, k)
                dve.scalar_tensor_tensor(xg, x[:, s, :], nmu[:, s:s + 1], gb[:, 0, :],
                                         ALU.add, ALU.mult).then_inc(xg_ready, 1)

            def norm_end(n, s):
                k = ST * n + s + 1
                dve.wait_ge(xg_ready, k)
                dve.wait_ge(rstd_ready, k)
                dve.scalar_tensor_tensor(x[:, s, :], xg, rstd[:, s:s + 1], gb[:, 1, :],
                                         ALU.mult, ALU.add).then_inc(x_ready, 1)

            def down(h0, order, u0, nch, n):
                m = nch - TAIL
                if m >= 2 * RING:
                    with dve.Fori(0, m // RING) as i:
                        for j in range(RING):
                            ht_low(h0, order, RING * i + (j + RING), j)
                    for j in range(m % RING):
                        ht_low(h0, order, m // RING * RING + j + RING, j)
                else:
                    for j in range(m):
                        ht_low(h0, order, j + RING, j)
                dve.wait_ge(gb_loaded, 32 * (n + 1))
                if n == 0:
                    dve.wait_ge(x_loaded, 16)
                for s in range(ST if n < 3 else ST - 1):
                    norm_start(n, s, u0 + nch)
                    norm_gain(n, s)
                    if s == 2 and n < 3:
                        xt_low(ST * (n + 1) + 1, 1)
                    norm_end(n, s)
                    if s in (1, 3) and n < 3:
                        xt_low(ST * (n + 1) + s - 1, s - 1)
                if n < 3:
                    xt_low(ST * (n + 1) + ST - 1, ST - 1)
                    return
                s = ST - 1
                halves = [slice(0, 512), slice(512, D)]
                for a, cs in enumerate(halves):
                    if a == 0:
                        dve.wait_ge(half_done, 1)
                    else:
                        dve.wait_ge(unit_done, UNITS)
                    dve.scalar_tensor_tensor(x[:, s, cs], x[:, s, cs], ALPHA, ps[:, 2 * s + a, :],
                                             ALU.mult, ALU.add).then_inc(z_ready, 1)
                    dve.wait_ge(z_ready, ST * n + ST + a)
                    dve.bn_stats(last_stat[:, 6 * a:6 * a + 6], x[:, s, cs]).then_inc(last_bn, 1)
                dve.wait_ge(last_bn, 2)
                dve.bn_aggr(last_stat[:, 12:14], last_stat[:, 0:12]).then_inc(last_var, 1)
                dve.wait_ge(last_var, 1)
                for a, cs in enumerate(halves):
                    dve.scalar_tensor_tensor(xg[:, cs], x[:, s, cs], last_stat[:, 12:13], gb[:, 0, cs],
                                             ALU.subtract, ALU.mult).then_inc(xg_ready, 1)
                dve.wait_ge(rstd_ready, 4 * ST)
                for a, cs in enumerate(halves):
                    dve.wait_ge(xg_ready, ST * n + ST + a)
                    dve.scalar_tensor_tensor(x[:, s, cs], xg[:, cs], rstd[:, s:s + 1], gb[:, 1, cs],
                                             ALU.mult, ALU.add).then_inc(x_ready, 1)

            def glu(l, conv0, free0, h0):
                def pair(i, q):
                    c = 2 * i + q
                    for e in range(2):
                        dve.wait_ge(conv_base, conv0 + 2 * c + e + 1)
                        dve.scalar_tensor_tensor(conv[:, q, e, 1:SEQ], ps[:, 2 * q + e, 0:SEQ - 1],
                                                 par(c + (col_ffn(l, 1) + e * FC)), conv[:, q, e, 1:SEQ],
                                                 ALU.mult, ALU.add).then_inc(tap1, 1)
                    for e in range(2):
                        dve.wait_ge(tap1, conv0 + 2 * c + e + 1)
                        dve.scalar_tensor_tensor(conv[:, q, e, 2:SEQ], ps[:, 2 * q + e, 0:SEQ - 2],
                                                 par(c + (col_ffn(l, 0) + e * FC)), conv[:, q, e, 2:SEQ],
                                                 ALU.mult, ALU.add).then_inc(bank_free, 1)
                    dve.wait_ge(bank_free, free0 + 2 * c + 2)
                    dve.wait_ge(gate_ready, FC * l + c + 1)
                    dve.tensor_tensor(h_at(c), act_g[:, q, :], conv[:, q, 1, :],
                                      ALU.mult).then_inc(h_ready, 1)

                with dve.Fori(0, FC // 2 - 1) as i:
                    pair(i, 0)
                    pair(i, 1)
                ht_first(h0, lambda j: j)
                pair(FC // 2 - 1, 0)
                pair(FC // 2 - 1, 1)

            for i in range(4):
                dve.wait_ge(xt_hi_ready, i + 1)
                dve.tensor_tensor(piece(xt_lo, i), piece(h, i), piece(xt_hi, i).bitcast(F32),
                                  ALU.subtract).then_inc(xt_ready, 1)
            dve.wait_ge(const_ready, 8)
            dve.reciprocal(inv_count[:, :], inv_count[:, :]).then_inc(inv_ready, 1)
            dve.wait_ge(inv_ready, 1)

            steps = 0
            for g in range(GROUPS):
                win = 2 << g
                here = slice(PAD, PAD + SEQ)
                u_buf = pool_buf[:, 0, here]
                dve.wait_ge(unit_done, U_POOLIN + g + 1)
                dve.tensor_copy(u_buf, ps[:, g, :]).then_inc(bank_free, 1)
                dve.wait_ge(bank_free, g + 1)
                src = 0
                for i in range(g + 1):
                    dst = 1 + i % 2
                    dve.tensor_tensor(pool_buf[:, dst, here], pool_buf[:, src, here],
                                      pool_buf[:, src, PAD - (1 << i):PAD + SEQ - (1 << i)],
                                      ALU.add).then_inc(pool_step, 1)
                    steps += 1
                    dve.wait_ge(pool_step, steps)
                    src = dst
                dve.scalar_tensor_tensor(pooled[:, g, :], pool_buf[:, src, here], 1.0 / win, u_buf,
                                         ALU.mult, ALU.subtract).then_inc(pool_step, 1)
                n = win - 1
                dve.tensor_tensor(pool_buf[:, 3 - src, PAD:PAD + n], pool_buf[:, src, PAD:PAD + n],
                                  inv_count[:, 0:n], ALU.mult).then_inc(pool_step, 1)
                steps += 2
                dve.wait_ge(pool_step, steps)
                dve.tensor_tensor(pooled[:, g, 0:n], pool_buf[:, 3 - src, PAD:PAD + n],
                                  pool_buf[:, 0, PAD:PAD + n], ALU.subtract).then_inc(pooled_ready, 1)
                dve.wait_ge(pooled_ready, g + 1)

            for s in (0, 1):
                dve.wait_ge(unit_done, U_Q)
                dve.tensor_copy(h[:, SLOT_V + s, :], ps[:, 4 + s, :]).then_inc(v_dve, 1)
            for j in range(AC):
                dve.wait_ge(unit_done, U_Q + j + 1)
                dve.tensor_scalar(h[:, SLOT_Q + j, :], ps[:, j, :], SCALE, None, ALU.mult).then_inc(bank_free, 1)

            def stage_q(p, e):
                half = slice(HEAD_DIM * e, HEAD_DIM * (e + 1))
                src = h[half, bass.ds(p + SLOT_Q, 1), :].rearrange("p a n -> p (a n)")
                dve.tensor_copy(q_hi[half, e, :], src).then_inc(q_high, 1)
                dve.wait_ge(q_high, 2 * p + e + 1)
                dve.tensor_tensor(q_lo[half, e, :], src, q_hi[half, e, :].bitcast(F32),
                                  ALU.subtract).then_inc(q_staged, 1)

            dve.wait_ge(bank_free, 8)
            stage_q(0, 0)
            stage_q(0, 1)
            for j in range(AC):
                dve.wait_ge(k_high, j + 1)
                dve.tensor_tensor(k_lo[:, j, :], ps[:, j, :], k_hi[:, j, :].bitcast(F32),
                                  ALU.subtract).then_inc(bank_free, 1)
            dve.wait_ge(table_loaded, 16)

            def mixed_out(g):
                dve.wait_ge(mixed_done, g + 1)
                dve.tensor_scalar(h[:, 4 + g, :], ps[:, 4 + g, :], table[:, COL_BPOOL + g:COL_BPOOL + g + 1],
                                  table[:, COL_PSCALE + g:COL_PSCALE + g + 1],
                                  ALU.add, ALU.mult).then_inc(h_ready, 1)

            for g in range(GROUPS - 1):
                mixed_out(g)

            def top(p, t):
                e, c = TILES[t % 8]
                dve.wait_ge(scores_done, 8 * p + t + 1)
                dve.reduce_max(neg_max[:, e, c:c + 1], ps[:, c, 0:P * (c + 1)], AX_X,
                               negate=True).then_inc(max_ready, 1)

            def move(p, t):
                e, c = TILES[t % 8]
                if c in (1, 2):
                    dve.wait_ge(pt_done, 8 * p + t + 1)
                    dve.tensor_copy(probs_t[:, p_off(c):p_off(c + 1)],
                                    ps[:, 4 + c % 2, 0:P * (c + 1)]).then_inc(pt_dve, 1)

            def head_out(p, e):
                dve.wait_ge(probs_ready, 8 * p + 4 * e + 4)
                dve.reciprocal(prob_inv[:, e, :], prob_sum[:, e, :]).then_inc(inv_sum, 1)
                dve.wait_ge(inv_sum, 2 * p + e + 1)
                dve.wait_ge(o_done, 2 * p + e + 1)
                dst = h[:, SLOT_O:SLOT_O + ST, bass.ds(P * p + HEAD_DIM * e, HEAD_DIM)]
                dve.tensor_tensor(dst, ps[:, 6 + e, 0:ST * HEAD_DIM].rearrange("p (c n) -> p c n", c=ST),
                                  prob_inv[:, e, :].unsqueeze(2).to_broadcast([P, ST, HEAD_DIM]),
                                  ALU.mult).then_inc(o_ready, 1)

            top(0, 0)
            for t in (1, 2, 3):
                top(0, t)
                if t == 2:
                    mixed_out(GROUPS - 1)
                move(0, t - 1)
            with dve.Fori(0, AC - 1) as p:
                for t in range(4, 12):
                    top(p, t)
                    move(p, t - 1)
                    if t == 4:
                        stage_q(p + 1, 0)
                    if t == 7:
                        head_out(p, 0)
                    if t == 8:
                        stage_q(p + 1, 1)
                    if t == 11:
                        head_out(p, 1)
            for t in range(4, 8):
                top(AC - 1, t)
                if t == 6:
                    ht_first(H_OUT0, lambda j: j + 4, (0,))
                move(AC - 1, t - 1)
            head_out(AC - 1, 0)
            head_out(AC - 1, 1)
            ht_first(H_OUT0, lambda j: j + 4, (1, 2, 3))
            for j in range(AC):
                dve.wait_ge(ot_done, j + 1)
                dve.tensor_copy(h[:, j, :], ps[:, j, :]).then_inc(h_ready, 1)

            down(H_OUT0, lambda j: (j + 4) % 8, U_OUT0, DC, 0)
            glu(0, CONV_UP0, FREE_UP0, H_DOWN0)
            down(H_DOWN0, lambda j: j, U_DOWN0, FC, 1)

            with dve.Fori(0, DC // 2) as i:
                for q in range(2):
                    c = 2 * i + q
                    dve.wait_ge(c_ready, c + 1)
                    dve.wait_ge(unit_done, U_CH + 2 * c + 2)
                    dve.tensor_tensor(conv[:, q, 1, :], ps[:, 2 * q + 1, :], conv[:, q, 0, :],
                                      ALU.mult).then_inc(bank_free, 2)
                    dve.wait_ge(conv_base, CONV_CH + c + 1)
                    dve.scalar_tensor_tensor(h_part(c, 1, SEQ), conv[:, q, 1, 0:SEQ - 1],
                                             par(c + (COL_ODDW + DC)), h_part(c, 1, SEQ),
                                             ALU.mult, ALU.add).then_inc(tap1, 1)
                    dve.wait_ge(tap1, CONV_CH + c + 1)
                    dve.scalar_tensor_tensor(h_part(c, 2, SEQ), conv[:, q, 1, 0:SEQ - 2],
                                             par(c + COL_ODDW), h_part(c, 2, SEQ),
                                             ALU.mult, ALU.add).then_inc(short_ready, 1)
            dve.wait_ge(short_ready, DC)
            for j in range(DC):
                if j == RING:
                    ht_first(H_OUT1, lambda j: j)
                dve.wait_ge(unit_done, U_B + j + 1)
                dve.tensor_tensor(h[:, j, :], ps[:, j % RING, :], h[:, j, :], ALU.mult).then_inc(h_ready, 1)
            down(H_OUT1, lambda j: j, U_OUT1, DC, 2)
            glu(1, CONV_UP1, FREE_UP1, H_DOWN1)
            down(H_DOWN1, lambda j: j, U_DOWN1, FC, 3)

        @block.tensor
        def _(pe):
            def three(dst, a_hi, a_lo, b_hi, b_lo, start, stop):
                pe.matmul(dst, a_hi, b_hi, start=start, stop=False)
                pe.matmul(dst, a_hi, b_lo, start=False, stop=False)
                return pe.matmul(dst, a_lo, b_hi, start=False, stop=stop)

            def x_transpose(s):
                for d in range(DC):
                    last = pe.transpose(ps[:, 2 * s + d // 4, (d % 4) * P:(d % 4 + 1) * P],
                                        x[:, s, d * P:(d + 1) * P], ident[:, :])
                last.then_inc(xt_ps, 1)

            def up_chunk(u0, j, bank, a, b, k):
                sl, ks = slot(u0 + j), slice(k * P, (k + 1) * P)
                return three(ps[:, bank, a:b], w_hi[:, sl, ks], w_lo[:, sl, ks],
                             xt_hi[:, k, a:b], xt_lo[:, k, a:b], k == 0, k == DC - 1)

            def up_part(u0, j, bank, a, b):
                for k in range(DC):
                    last = up_chunk(u0, j, bank, a, b, k)
                return last

            def up_unit(u0, i, j, bank):
                pe.wait_ge(split_ready, u0 + RING * i + (j + 1))
                up_part(u0, j, bank, 0, SEQ).then_inc(unit_done, 1)

            def next_up(u0, n):
                pe.wait_ge(xt_ready, ST * (n + 1) + 2)
                for j in range(RING):
                    pe.wait_ge(split_ready, u0 + j + 1)
                    up_part(u0, j, j, 0, SEQ // 2)
                    if j in (0, 2):
                        pe.wait_ge(x_ready, ST * n + 3 + j // 2)
                        x_transpose(2 + j // 2)
                pe.wait_ge(xt_ready, ST * (n + 2))
                for j in range(RING):
                    up_part(u0, j, j, SEQ // 2, SEQ).then_inc(unit_done, 1)

            def down_part(sl, j, s, start, stop, halves=(0, 1)):
                ss = slice(s * P, (s + 1) * P)
                for n in halves:
                    ns = slice(n * 512, (n + 1) * 512)
                    last = three(ps[:, 2 * s + n, :], ht_hi[:, j, ss], ht_lo[:, j, ss],
                                 w_hi[:, sl, ns], w_lo[:, sl, ns], start, stop)
                return last

            def down(h0, u0, nch, n, banks_read, begun=False):
                def unit(i, j):
                    pe.wait_ge(split_ready, u0 + RING * i + (j + 1))
                    pe.wait_ge(ht_ready, h0 + RING * i + (j + 1))
                    for s in range(ST):
                        last = down_part(slot(u0 + j), j, s, False, False)
                    last.then_inc(unit_done, 1)

                m = nch - TAIL
                for j in range(2):
                    pe.wait_ge(split_ready, u0 + j + 1)
                    pe.wait_ge(ht_ready, h0 + j + 1)
                    for s in ((3,) if begun and j == 0 else (2, 3)):
                        down_part(slot(u0 + j), j, s, j == 0, False)
                read_sem, reads = banks_read
                pe.wait_ge(read_sem, reads)
                for j in range(2):
                    for s in (0, 1):
                        last = down_part(slot(u0 + j), j, s, j == 0, False)
                    last.then_inc(unit_done, 1)
                unit(0, 2)
                unit(0, 3)
                if m >= 2 * RING:
                    with pe.Fori(1, m // RING) as i:
                        for j in range(RING):
                            unit(i, j)
                    for j in range(m % RING):
                        unit(m // RING, j)
                for s in range(ST if n < 3 else ST - 1):
                    for j in range(m, nch):
                        if s == 0:
                            pe.wait_ge(split_ready, u0 + j + 1)
                            pe.wait_ge(ht_ready, h0 + j + 1)
                        last = down_part(slot(u0 + j), j % RING, s, False, j == nch - 1)
                        if s == ST - 1:
                            last.then_inc(unit_done, 1)
                        if s >= 2 and j == m and n < 3:
                            pe.wait_ge(x_ready, ST * n + s - 1)
                            x_transpose(s - 2)
                    if s < ST - 1:
                        last.then_inc(tile_done, 1)
                if n == 3:
                    for half in range(2):
                        for j in range(m, nch):
                            last = down_part(slot(u0 + j), j % RING, ST - 1, False, j == nch - 1, (half,))
                            if half:
                                last.then_inc(unit_done, 1)
                        if not half:
                            last.then_inc(half_done, 1)

            def glu(u0, free0, n):
                next_up(u0, n)
                with pe.Fori(1, FC // 2) as i:
                    for j in range(RING):
                        pe.wait_ge(bank_free, RING * i + (free0 + j + 1 - RING))
                        up_unit(u0, i, j, j)

            for j in range(2):
                pe.wait_ge(split_ready, j + 1)
                for k in range(DC):
                    if j == 0 and k in (0, DC // 2):
                        pe.wait_ge(xt_ready, 1 + k // (DC // 2))
                    up_chunk(U_POOLIN, j, j, 0, SEQ // 2, k)
            pe.wait_ge(xt_ready, ST)
            for j in range(2):
                up_part(U_POOLIN, j, j, SEQ // 2, SEQ).then_inc(unit_done, 1)
            for j in range(2, RING):
                up_unit(U_POOLIN, 0, j, j)

            for j in range(4):
                pe.wait_ge(split_ready, U_V + j + 1)
                for s in range(ST):
                    ss = slice(s * P, (s + 1) * P)
                    for kk in range(2):
                        ns = slice(kk * ATT, (kk + 1) * ATT)
                        k = 2 * j + kk
                        last = three(ps[:, 4 + s, :], xt_hi[:, k, ss], xt_lo[:, k, ss],
                                     w_hi[:, j, ns], w_lo[:, j, ns], k == 0, k == DC - 1)
                last.then_inc(unit_done, 1)
            with pe.Fori(0, 2) as i:
                for j in range(RING):
                    pe.wait_ge(bank_free, RING * i + j + 1)
                    up_unit(U_Q, i, j, j)
            pe.wait_ge(wpool_loaded, 16)
            pe.wait_ge(v_dve, 2)
            pe.wait_ge(v_ready, 2)
            def mix(g):
                pe.wait_ge(pooled_ready, g + 1)
                pe.matmul(ps[:, 4 + g, :], wpool[:, g, :], pooled[:, g, :], start=True, stop=True
                          ).then_inc(mixed_done, 1)

            for g in range(GROUPS - 1):
                mix(g)

            def scores(p, t):
                e, c = TILES[t % 8]
                width = P * (c + 1)
                qs = slice(c * P, (c + 1) * P)
                pair = bass.ds(p + t // 8, 1)
                three(ps[:, c, 0:width], q_hi[:, e, qs], q_lo[:, e, qs],
                      k_hi[:, pair, 0:width].rearrange("p a n -> p (a n)"),
                      k_lo[:, pair, 0:width].rearrange("p a n -> p (a n)"), True, False)
                pe.matmul(ps[:, c, c * P:width], ident_b[:, :], mask_b[:, :],
                          start=False, stop=True).then_inc(scores_done, 1)

            def transposed(p, t):
                e, c = TILES[t % 8]
                pe.wait_ge(probs_ready, 8 * p + t + 1)
                for kc in range(c + 1):
                    last = pe.transpose(ps[:, 4 + c % 2, kc * P:(kc + 1) * P],
                                        probs[:, e, p_off(c) + kc * P:p_off(c) + (kc + 1) * P], ident[:, :])
                last.then_inc(pt_done, 1)

            def outputs(p, t):
                e, c = TILES[t]
                if c in (0, 3):
                    pe.wait_ge(pt_act, 4 * p + 2 * e + (1 if c == 0 else 2))
                else:
                    pe.wait_ge(pt_dve, 4 * p + 2 * e + c)
                for kc in range(c + 1):
                    at = p_off(c) + kc * P
                    last = pe.matmul(ps[:, 6 + e, c * HEAD_DIM:(c + 1) * HEAD_DIM], probs_t[:, at:at + P],
                                     h[:, SLOT_V + kc, bass.ds(P * p + HEAD_DIM * e, HEAD_DIM)],
                                     start=(kc == 0), stop=(kc == c))
                if c == ST - 1:
                    last.then_inc(o_done, 1)

            def step(p, t, more):
                if t + 3 < 8 or more:
                    if (t + 3) % 4 == 0:
                        pe.wait_ge(q_staged, 2 * p + (t + 3) // 4 + 1)
                    scores(p, t + 3)
                transposed(p, t)
                outputs(p, t - 1)

            def o_transpose(j):
                pe.wait_ge(o_ready, 2 * (j + 1))
                for s in range(ST):
                    last = pe.transpose(ps[:, j, s * P:(s + 1) * P], o_nat[:, s, j * P:(j + 1) * P], ident[:, :])
                last.then_inc(ot_done, 1)

            pe.wait_ge(const_ready, 3)
            pe.wait_ge(q_staged, 1)
            pe.wait_ge(bank_free, 12)
            for t in range(4):
                scores(0, t)
            mix(GROUPS - 1)
            pe.wait_ge(h_ready, GROUPS - 1)
            transposed(0, 0)
            with pe.Fori(0, AC - 1) as p:
                for t in range(1, 9):
                    step(p, t, True)

            for t in range(1, 8):
                step(AC - 1, t, False)
                if t >= 5:
                    o_transpose(t - 5)
            pe.wait_ge(split_ready, U_OUT0 + 1)
            pe.wait_ge(ht_ready, H_OUT0 + 1)
            down_part(slot(U_OUT0), 0, 2, True, False, (0,))
            outputs(AC - 1, 7)
            down_part(slot(U_OUT0), 0, 2, True, False, (1,))
            o_transpose(AC - 1)

            down(H_OUT0, U_OUT0, DC, 0, (h_ready, H_DOWN0), begun=True)
            glu(U_UP0, FREE_UP0, 0)
            down(H_DOWN0, U_DOWN0, FC, 1, (bank_free, FREE_CH))
            next_up(U_CH, 1)
            with pe.Fori(1, DC // 2) as i:
                for j in range(RING):
                    pe.wait_ge(bank_free, RING * i + (FREE_CH + 2 * (j // 2) - 2))
                    up_unit(U_CH, i, j, j)
            for j in range(DC):
                if j < RING:
                    pe.wait_ge(bank_free, FREE_UP1 - 2 + j // 2 * 2)
                else:
                    pe.wait_ge(h_ready, H_OUT1 + j - RING + 1)
                up_unit(U_B, 0, j, j % RING)
            down(H_OUT1, U_OUT1, DC, 2, (h_ready, H_DOWN1))
            glu(U_UP1, FREE_UP1, 2)
            down(H_DOWN1, U_DOWN1, FC, 3, (bank_free, FREE_END))


def kernel(x, even_w_in, even_w_pool, even_b_pool, even_pool_scale, even_w_out,
           odd_w_in, odd_conv_w, odd_conv_b, odd_w_out, mix_ln_g, mix_ln_b,
           ffn_w_up, ffn_conv_w, ffn_conv_b, ffn_w_down, ffn_ln_g, ffn_ln_b):
    import numpy as _np
    import concourse.bacc as _bacc
    from concourse import mybir as _mybir
    from concourse.bass_utils import run_bass_kernel_spmd as _run

    (x, even_w_in, even_w_pool, even_b_pool, even_pool_scale, even_w_out, odd_w_in, odd_conv_w, odd_conv_b,
     odd_w_out, mix_ln_g, mix_ln_b, ffn_w_up, ffn_conv_w, ffn_conv_b, ffn_w_down, ffn_ln_g, ffn_ln_b) = map(
        _np.asarray, (x, even_w_in, even_w_pool, even_b_pool, even_pool_scale, even_w_out, odd_w_in, odd_conv_w,
                      odd_conv_b, odd_w_out, mix_ln_g, mix_ln_b, ffn_w_up, ffn_conv_w, ffn_conv_b, ffn_w_down,
                      ffn_ln_g, ffn_ln_b))
    seq, d = x.shape[1:]
    dc, ff, att = d // P, ffn_w_down.shape[1], d // 2
    fc = ff // P

    def by_cols(w):
        return w.reshape(dc, P, -1, P).transpose(2, 1, 0, 3).reshape(-1, P, d)

    def by_rows(w):
        return w.reshape(-1, P, d)

    def pairs(a, b):
        return _np.stack([a, b], axis=1).reshape(-1, P, d)

    def ffn(l):
        up = by_cols(ffn_w_up[l])
        return [pairs(up[:fc], up[fc:]), by_rows(ffn_w_down[l])]

    even, odd, even_out = by_cols(even_w_in[0]), by_cols(odd_w_in[0]), by_rows(even_w_out[0])
    ac = att // P
    v = even_w_in[0][:, 2 * att:3 * att].reshape(dc // 2, 2, P, att).transpose(0, 2, 1, 3).reshape(-1, P, d)
    units = _np.concatenate(
        [even[3 * ac:], v, even[:2 * ac], even_out[ac:], even_out[:ac]] + ffn(0)
        + [pairs(odd[dc:2 * dc], odd[2 * dc:]), odd[:dc], by_rows(odd_w_out[0])] + ffn(1))
    table = _np.concatenate(
        [a.reshape(-1, P) for l in range(mix_ln_g.shape[0]) for a in (ffn_conv_w[l], ffn_conv_b[l])]
        + [a.reshape(-1, P) for a in (even_b_pool, even_pool_scale, odd_conv_w, odd_conv_b)]).T
    ln = _np.stack([mix_ln_g, mix_ln_b, ffn_ln_g, ffn_ln_b], axis=1).reshape(-1, 2, d)
    arrays = {
        "x_in": x[0],
        "xt_in": x[0].reshape(2, seq // 2, 2, dc // 2, P).transpose(0, 2, 4, 3, 1),
        "units": units,
        "wpool_in": even_w_pool[0].reshape(-1, P, P).transpose(1, 0, 2),
        "table_in": table,
        "ln_in": ln,
    }
    arrays = {k: _np.ascontiguousarray(a) for k, a in arrays.items()}
    nc = _bacc.Bacc("TRN2", target_bir_lowering=False, num_devices=1)
    args = [nc.dram_tensor(k, a.shape, _mybir.dt.from_np(a.dtype), kind="ExternalInput").ap()
            for k, a in arrays.items()]
    out = nc.dram_tensor("out", (seq, d), _mybir.dt.float32, kind="ExternalOutput").ap()
    trunk_program(nc, fc, *args, out)
    return _run(nc, [arrays], core_ids=[0]).results[0]["out"].reshape(1, seq, d)
```
